# Optimizing a Trainium2 kernel written in Bass

```python
import math
import jax, jax.numpy as jnp
from jax import lax
import numpy as np

D_MODEL = 1024
BATCH = 1
SEQ = 128
DEPTH = 1
DEC_BATCH = 1
DEC_SEQ = 256
PAST_LEN = 128

GRID_W = 64
D_GROUP = 512
N_MIXERS = 3
D_MIX = N_MIXERS * D_GROUP
LRU_BLOCKS = 8
LRU_BLOCK = D_GROUP // LRU_BLOCKS
CONV_W = 4
CONV_PAD = (2, 1)
LRU_C = 8.0
HG_HEADS = 4
HG_DK = D_GROUP // HG_HEADS
HG_DV = D_GROUP // HG_HEADS
HG_CHUNK = 16
ML_HEADS = 4
ML_DH = D_GROUP // ML_HEADS
ML_CHUNK = 64
N_EXPERTS = 16
N_GROUPS = 4
EXPERTS_PER_GROUP = N_EXPERTS // N_GROUPS
TOP_K = 2
D_FF = 512
ALPHA = (2.0 * DEPTH) ** 0.25
BETA = (8.0 * DEPTH) ** -0.25
EPS = 1e-5
NEG = -1e30
TINY = 1e-30
IN_COLS = (D_GROUP,) * 11 + (4 * ML_HEADS,)
D_IN = sum(IN_COLS)
IN_SPLITS = tuple(sum(IN_COLS[:i + 1]) for i in range(len(IN_COLS) - 1))
ML_GATE_OFF = D_IN - 4 * ML_HEADS

kernel_name = 'hybrid_rglru_hgrn2_mlstm_moe_diffusion_step'

def _layer_norm(x, g, b):
    xf = x.astype(jnp.float32)
    mu = jnp.mean(xf, -1, keepdims=True)
    var = jnp.mean(jnp.square(xf - mu), -1, keepdims=True)
    return ((xf - mu) * lax.rsqrt(var + EPS) * g + b).astype(x.dtype)

def _head_rms(x, g):
    y = x * lax.rsqrt(jnp.mean(jnp.square(x), -1, keepdims=True) + EPS)
    return y.reshape(x.shape[0], x.shape[1], -1) * g

def _head_ln(x, g):
    mu = jnp.mean(x, -1, keepdims=True)
    var = jnp.mean(jnp.square(x - mu), -1, keepdims=True)
    y = (x - mu) * lax.rsqrt(var + EPS)
    return y.reshape(x.shape[0], x.shape[1], -1) * g

def _grid_pos_embed(n_tokens):
    rows = n_tokens // GRID_W
    r = jnp.repeat(jnp.arange(rows, dtype=jnp.float32), GRID_W)
    c = jnp.tile(jnp.arange(GRID_W, dtype=jnp.float32), rows)
    q = D_MODEL // 4
    freq = jnp.exp(-math.log(10000.0) * jnp.arange(q, dtype=jnp.float32) / q)
    ar = r[:, None] * freq
    ac = c[:, None] * freq
    return jnp.concatenate([jnp.sin(ar), jnp.cos(ar), jnp.sin(ac), jnp.cos(ac)], axis=-1)

def _dwconv(x, w, b):
    y = lax.conv_general_dilated(x, w.astype(x.dtype)[:, None, :], (1,), [CONV_PAD],
                                 dimension_numbers=('NWC', 'WIO', 'NWC'),
                                 feature_group_count=x.shape[-1])
    return y + b.astype(x.dtype)

def _rglru_dir(x, w_a, b_a, w_x, b_x, lam, h0):
    B, T, _ = x.shape
    xb = x.reshape(B, T, LRU_BLOCKS, LRU_BLOCK)
    r = jax.nn.sigmoid(jnp.einsum('btnd,nde->btne', xb, w_a).reshape(B, T, D_GROUP) + b_a)
    i = jax.nn.sigmoid(jnp.einsum('btnd,nde->btne', xb, w_x).reshape(B, T, D_GROUP) + b_x)
    log_a = -LRU_C * r * jax.nn.softplus(-lam)
    a = jnp.exp(log_a)
    u = jnp.sqrt(jnp.maximum(-jnp.expm1(2.0 * log_a), 0.0)) * (i * x)

    def combine(p, q):
        return p[0] * q[0], q[0] * p[1] + q[1]

    a_cum, h = lax.associative_scan(combine, (a, u), axis=1)
    h = h + a_cum * h0[:, None, :]
    return h, h[:, -1]

def _hgrn2_dir(q, k, v, log_f, S0):
    B, T, H, _ = q.shape
    n = T // HG_CHUNK
    rs = lambda z: z.reshape(B, n, HG_CHUNK, H, z.shape[-1])
    q, k, v, log_f = rs(q), rs(k), rs(v), rs(log_f)
    b = jnp.cumsum(log_f, axis=2)
    causal = jnp.tril(jnp.ones((HG_CHUNK, HG_CHUNK), bool))[None, None, :, :, None, None]
    diff = b[:, :, :, None] - b[:, :, None, :]
    decay = jnp.exp(jnp.where(causal, diff, NEG))
    A = jnp.einsum('bnthd,bnshd,bntshd->bnhts', q, k, decay)
    o_intra = jnp.einsum('bnhts,bnshe->bnthe', A, v)
    b_last = b[:, :, -1]
    k_dec = k * jnp.exp(b_last[:, :, None] - b)
    dS = jnp.einsum('bnshd,bnshe->bnhde', k_dec, v)

    def step(S, inp):
        dec, ds = inp
        return dec[..., None] * S + ds, S

    S_final, S_start = lax.scan(step, S0, (jnp.moveaxis(jnp.exp(b_last), 1, 0), jnp.moveaxis(dS, 1, 0)))
    S_start = jnp.moveaxis(S_start, 0, 1)
    o_inter = jnp.einsum('bnthd,bnhde->bnthe', q * jnp.exp(b), S_start)
    return (o_intra + o_inter).reshape(B, T, H, -1), S_final

def _mlstm_dir(q, k, v, log_i, log_f, C0, n0, m0):
    B, T, H, DH = q.shape
    n = T // ML_CHUNK
    L = ML_CHUNK
    rs = lambda z: z.reshape((B, n, L) + z.shape[2:])
    q, k, v, log_i, log_f = rs(q), rs(k), rs(v), rs(log_i), rs(log_f)
    b = jnp.cumsum(log_f, axis=2)
    b_last = b[:, :, -1]
    w_state = b_last[:, :, None] - b + log_i
    m_loc = jnp.max(w_state, axis=2)
    e_state = jnp.exp(w_state - m_loc[:, :, None])
    dC = jnp.einsum('bnsh,bnshd,bnshe->bnhde', e_state, k, v)
    dn = jnp.einsum('bnsh,bnshd->bnhd', e_state, k)

    def step(carry, inp):
        C, nn, m = carry
        bl, ml, dc, dnn = inp
        m_new = jnp.maximum(bl + m, ml)
        s_old = jnp.exp(bl + m - m_new)
        s_new = jnp.exp(ml - m_new)
        C_new = s_old[..., None, None] * C + s_new[..., None, None] * dc
        n_new = s_old[..., None] * nn + s_new[..., None] * dnn
        return (C_new, n_new, m_new), (C, nn, m)

    mv = lambda z: jnp.moveaxis(z, 1, 0)
    (C_f, n_f, m_f), (C_s, n_s, m_s) = lax.scan(step, (C0, n0, m0), (mv(b_last), mv(m_loc), mv(dC), mv(dn)))
    C_s, n_s, m_s = jnp.moveaxis(C_s, 0, 1), jnp.moveaxis(n_s, 0, 1), jnp.moveaxis(m_s, 0, 1)
    causal = jnp.tril(jnp.ones((L, L), bool))[None, None, :, :, None]
    D = jnp.where(causal, b[:, :, :, None, :] - b[:, :, None, :, :] + log_i[:, :, None, :, :], NEG)
    inter = b + m_s[:, :, None]
    m_t = jnp.maximum(inter, jnp.max(D, axis=3))
    P = jnp.exp(D - m_t[:, :, :, None])
    s_inter = jnp.exp(inter - m_t)
    W = P * jnp.einsum('bnthd,bnshd->bntsh', q, k)
    num = jnp.einsum('bntsh,bnshe->bnthe', W, v) + s_inter[..., None] * jnp.einsum('bnthd,bnhde->bnthe', q, C_s)
    den = jnp.sum(W, axis=3) + s_inter * jnp.einsum('bnthd,bnhd->bnth', q, n_s)
    h = num / jnp.maximum(jnp.abs(den), jnp.exp(-m_t))[..., None]
    return h.reshape(B, T, H, DH), (C_f, n_f, m_f)

def _mixer(h, init, w_in, b_in, conv_w, conv_b, lru_wa, lru_ba, lru_wx, lru_bx, lru_lam,
           hg_lower, hg_norm_g, ml_norm_g, w_out):
    B, T, _ = h.shape
    f32 = jnp.float32
    z = (jnp.einsum('btd,de->bte', h, w_in) + b_in).astype(f32)
    (r_x, r_g, g_q, g_ff, g_fb, g_i, g_o, m_q, m_k, m_v, m_o, m_g) = jnp.split(z, IN_SPLITS, axis=-1)
    h0, S0, C0, n0, m0 = [s.astype(f32) for s in init]
    flip = lambda a: jnp.flip(a, axis=1)
    heads = lambda a, H: a.reshape(B, T, H, -1)
    xc = _dwconv(r_x, conv_w, conv_b)
    o_f, hT_f = _rglru_dir(xc, lru_wa[0], lru_ba[0], lru_wx[0], lru_bx[0], lru_lam[0], h0[:, 0])
    o_b, hT_b = _rglru_dir(flip(xc), lru_wa[1], lru_ba[1], lru_wx[1], lru_bx[1], lru_lam[1], h0[:, 1])
    y_r = jax.nn.gelu(r_g) * (o_f + flip(o_b))
    q_h = heads(jax.nn.silu(g_q), HG_HEADS)
    v_h = heads(g_i, HG_HEADS)

    def forget(pre, lb):
        sig = jax.nn.sigmoid(pre)
        log_f = jnp.log(jnp.maximum(lb + (1.0 - lb) * sig, TINY))
        kk = (1.0 - lb) * (1.0 - sig)
        return heads(log_f, HG_HEADS), heads(kk, HG_HEADS)

    lf_f, k_f = forget(g_ff, hg_lower[0])
    lf_b, k_b = forget(g_fb, hg_lower[1])
    s_f, ST_f = _hgrn2_dir(q_h, k_f, v_h, lf_f, S0[:, 0])
    s_b, ST_b = _hgrn2_dir(flip(q_h), flip(k_b), flip(v_h), flip(lf_b), S0[:, 1])
    y_h = _head_rms(s_f + flip(s_b), hg_norm_g) * jax.nn.silu(g_o)
    mq = heads(m_q, ML_HEADS)
    mk = heads(m_k, ML_HEADS) * ML_DH ** -0.5
    mvv = heads(m_v, ML_HEADS)
    mg = m_g.reshape(B, T, 2, 2, ML_HEADS)
    log_i = mg[:, :, :, 0]
    log_fm = jax.nn.log_sigmoid(mg[:, :, :, 1])
    c_f, (CT_f, nT_f, mT_f) = _mlstm_dir(mq, mk, mvv, log_i[:, :, 0], log_fm[:, :, 0], C0[:, 0], n0[:, 0], m0[:, 0])
    c_b, (CT_b, nT_b, mT_b) = _mlstm_dir(flip(mq), flip(mk), flip(mvv), flip(log_i[:, :, 1]), flip(log_fm[:, :, 1]),
                                         C0[:, 1], n0[:, 1], m0[:, 1])
    y_m = jax.nn.sigmoid(m_o) * _head_ln(c_f + flip(c_b), ml_norm_g)
    y = jnp.concatenate([y_r, y_h, y_m], axis=-1).astype(h.dtype)
    out = jnp.einsum('bte,ed->btd', y, w_out)
    finals = (jnp.stack([hT_f, hT_b], 1), jnp.stack([ST_f, ST_b], 1), jnp.stack([CT_f, CT_b], 1),
              jnp.stack([nT_f, nT_b], 1), jnp.stack([mT_f, mT_b], 1))
    return out, finals

def _moe(h, w_router, b_router, w_gate, w_up, w_down):
    f32 = jnp.float32
    scores = jax.nn.softmax(jnp.einsum('btd,de->bte', h, w_router).astype(f32), axis=-1)
    sel = (scores + b_router.astype(f32)).reshape(scores.shape[:-1] + (N_GROUPS, EXPERTS_PER_GROUP))
    grp_score = jnp.sum(lax.top_k(sel, TOP_K)[0], axis=-1)
    best = jnp.argmax(grp_score, axis=-1)[..., None] == jnp.arange(N_GROUPS)
    masked = jnp.where(best[..., None], sel, NEG).reshape(scores.shape)
    _, idx = lax.top_k(masked, TOP_K)
    w = jnp.take_along_axis(scores, idx, axis=-1)
    w = w / jnp.sum(w, -1, keepdims=True)
    combine = jnp.sum((idx[..., None] == jnp.arange(N_EXPERTS)).astype(f32) * w[..., None], axis=-2)
    hg = jnp.einsum('btd,edf->btef', h, w_gate)
    hu = jnp.einsum('btd,edf->btef', h, w_up)
    act = jax.nn.silu(hg) * hu * combine[..., None].astype(h.dtype)
    return jnp.einsum('btef,efd->btd', act, w_down)

def _layer(x, mod, init, w_in, b_in, conv_w, conv_b, lru_wa, lru_ba, lru_wx, lru_bx, lru_lam,
           hg_lower, hg_norm_g, ml_norm_g, w_out, ln1_g, ln1_b, ln2_g, ln2_b,
           w_router, b_router, w_gate, w_up, w_down):
    sh1, sc1, g1, sh2, sc2, g2 = jnp.split(mod.astype(x.dtype), 6, axis=-1)
    y, finals = _mixer(x * (1 + sc1) + sh1, init, w_in, b_in, conv_w, conv_b, lru_wa, lru_ba, lru_wx, lru_bx,
                       lru_lam, hg_lower, hg_norm_g, ml_norm_g, w_out)
    x = _layer_norm(ALPHA * x + g1 * y, ln1_g, ln1_b)
    f = _moe(x * (1 + sc2) + sh2, w_router, b_router, w_gate, w_up, w_down)
    x = _layer_norm(ALPHA * x + g2 * f, ln2_g, ln2_b)
    return x, finals

def setup_inputs(seed: int = 0) -> dict:
    key = jax.random.key(seed)
    ks = iter(jax.random.split(key, 40))
    f32 = jnp.float32
    nrm = lambda shape, scale: scale * jax.random.normal(next(ks), shape, f32)
    x_prompt = nrm((BATCH, SEQ, D_MODEL), 1.0)
    x_sample = nrm((DEC_BATCH, DEC_SEQ, D_MODEL), 1.0)
    state_lru_h = nrm((DEC_BATCH, DEPTH, 2, D_GROUP), 0.5)
    state_hgrn_S = nrm((DEC_BATCH, DEPTH, 2, HG_HEADS, HG_DK, HG_DV), 0.5)
    state_mlstm_C = nrm((DEC_BATCH, DEPTH, 2, ML_HEADS, ML_DH, ML_DH), 0.1)
    state_mlstm_n = jnp.abs(nrm((DEC_BATCH, DEPTH, 2, ML_HEADS, ML_DH), 0.3))
    state_mlstm_m = nrm((DEC_BATCH, DEPTH, 2, ML_HEADS), 1.0)
    c = nrm((DEC_BATCH, D_MODEL), 1.0)
    c_ctx = nrm((D_MODEL,), 1.0)
    w_ada = nrm((DEPTH, D_MODEL, 6 * D_MODEL), D_MODEL ** -0.5)
    b_ada = nrm((DEPTH, 6 * D_MODEL), 0.02)
    w_in = nrm((DEPTH, D_MODEL, D_IN), D_MODEL ** -0.5)
    gate_bias = jnp.zeros((2, 2, ML_HEADS), f32).at[:, 1].set(jnp.linspace(3.0, 6.0, ML_HEADS)).reshape(-1)
    b_in = nrm((DEPTH, D_IN), 0.02).at[:, ML_GATE_OFF:].add(gate_bias)
    conv_w = nrm((DEPTH, CONV_W, D_GROUP), CONV_W ** -0.5)
    conv_b = nrm((DEPTH, D_GROUP), 0.02)
    lru_wa = nrm((DEPTH, 2, LRU_BLOCKS, LRU_BLOCK, LRU_BLOCK), LRU_BLOCK ** -0.5)
    lru_ba = nrm((DEPTH, 2, D_GROUP), 0.02)
    lru_wx = nrm((DEPTH, 2, LRU_BLOCKS, LRU_BLOCK, LRU_BLOCK), LRU_BLOCK ** -0.5)
    lru_bx = nrm((DEPTH, 2, D_GROUP), 0.02)
    a8 = jax.random.uniform(next(ks), (DEPTH, 2, D_GROUP), f32, 0.9, 0.999)
    a1 = a8 ** (1.0 / LRU_C)
    lru_lam = jnp.log(a1) - jnp.log1p(-a1)
    hg_lb = nrm((DEPTH, 2, D_GROUP), 1.0)
    hg_norm_g = 1.0 + nrm((DEPTH, D_GROUP), 0.02)
    ml_norm_g = 1.0 + nrm((DEPTH, D_GROUP), 0.02)
    w_out = nrm((DEPTH, D_MIX, D_MODEL), BETA * D_MIX ** -0.5)
    ln1_g = 1.0 + nrm((DEPTH, D_MODEL), 0.02)
    ln1_b = nrm((DEPTH, D_MODEL), 0.02)
    ln2_g = 1.0 + nrm((DEPTH, D_MODEL), 0.02)
    ln2_b = nrm((DEPTH, D_MODEL), 0.02)
    w_router = nrm((D_MODEL, N_EXPERTS), D_MODEL ** -0.5)
    b_router = nrm((N_EXPERTS,), 0.01)
    w_gate = nrm((DEPTH, N_EXPERTS, D_MODEL, D_FF), D_MODEL ** -0.5)
    w_up = nrm((DEPTH, N_EXPERTS, D_MODEL, D_FF), D_MODEL ** -0.5)
    w_down = nrm((DEPTH, N_EXPERTS, D_FF, D_MODEL), BETA * D_FF ** -0.5)
    return {'x_prompt': x_prompt, 'x_sample': x_sample,
            'state_lru_h': state_lru_h, 'state_hgrn_S': state_hgrn_S, 'state_mlstm_C': state_mlstm_C,
            'state_mlstm_n': state_mlstm_n, 'state_mlstm_m': state_mlstm_m,
            'c': c, 'c_ctx': c_ctx, 'w_ada': w_ada, 'b_ada': b_ada, 'w_in': w_in, 'b_in': b_in,
            'conv_w': conv_w, 'conv_b': conv_b, 'lru_wa': lru_wa, 'lru_ba': lru_ba, 'lru_wx': lru_wx,
            'lru_bx': lru_bx, 'lru_lam': lru_lam, 'hg_lb': hg_lb, 'hg_norm_g': hg_norm_g, 'ml_norm_g': ml_norm_g,
            'w_out': w_out, 'ln1_g': ln1_g, 'ln1_b': ln1_b, 'ln2_g': ln2_g, 'ln2_b': ln2_b,
            'w_router': w_router, 'b_router': b_router, 'w_gate': w_gate, 'w_up': w_up, 'w_down': w_down}

def reference(x_prompt, x_sample, state_lru_h, state_hgrn_S, state_mlstm_C, state_mlstm_n, state_mlstm_m,
              c, c_ctx, w_ada, b_ada, w_in, b_in, conv_w, conv_b, lru_wa, lru_ba, lru_wx, lru_bx, lru_lam,
              hg_lb, hg_norm_g, ml_norm_g, w_out, ln1_g, ln1_b, ln2_g, ln2_b,
              w_router, b_router, w_gate, w_up, w_down):
    f32 = jnp.float32
    Bp = x_prompt.shape[0]
    lb_soft = jax.nn.softmax(hg_lb.astype(f32), axis=0)
    hg_lower = jnp.cumsum(lb_soft, axis=0) - lb_soft[0:1]
    mod_ctx = jnp.einsum('d,lde->le', jax.nn.silu(c_ctx), w_ada) + b_ada
    mod_lat = jnp.einsum('bd,lde->lbe', jax.nn.silu(c), w_ada) + b_ada[:, None]
    init_ctx = (jnp.zeros((Bp, 2, D_GROUP), f32),
                jnp.zeros((Bp, 2, HG_HEADS, HG_DK, HG_DV), f32),
                jnp.zeros((Bp, 2, ML_HEADS, ML_DH, ML_DH), f32),
                jnp.zeros((Bp, 2, ML_HEADS, ML_DH), f32),
                jnp.zeros((Bp, 2, ML_HEADS), f32))
    xp = x_prompt
    xs = x_sample + _grid_pos_embed(x_sample.shape[1]).astype(x_sample.dtype)
    fin_h, fin_S, fin_C, fin_n, fin_m = [], [], [], [], []
    for l in range(DEPTH):
        lp = (w_in[l], b_in[l], conv_w[l], conv_b[l], lru_wa[l], lru_ba[l], lru_wx[l], lru_bx[l], lru_lam[l],
              hg_lower[l], hg_norm_g[l], ml_norm_g[l], w_out[l], ln1_g[l], ln1_b[l], ln2_g[l], ln2_b[l],
              w_router, b_router, w_gate[l], w_up[l], w_down[l])
        xp, (h_l, S_l, C_l, n_l, m_l) = _layer(xp, mod_ctx[l][None, None], init_ctx, *lp)
        fin_h.append(h_l)
        fin_S.append(S_l)
        fin_C.append(C_l)
        fin_n.append(n_l)
        fin_m.append(m_l)
        init_lat = (state_lru_h[:, l], state_hgrn_S[:, l], state_mlstm_C[:, l], state_mlstm_n[:, l], state_mlstm_m[:, l])
        xs, _ = _layer(xs, mod_lat[l][:, None], init_lat, *lp)
    return (xp, xs, jnp.stack(fin_h, 1), jnp.stack(fin_S, 1), jnp.stack(fin_C, 1),
            jnp.stack(fin_n, 1), jnp.stack(fin_m, 1))


_drawn_inputs = setup_inputs


def setup_inputs(seed=0):
    import zlib

    import numpy as np

    out = dict(_drawn_inputs(seed))
    spreads = {}
    factors = {'state_hgrn_S': 38.574,
     'state_mlstm_C': 8.0,
     'state_mlstm_n': 8.0,
     'state_mlstm_m': 3.233,
     'lru_ba': 8.0,
     'lru_bx': 8.0,
     'hg_norm_g': 4.226,
     'ml_norm_g': 8.0,
     'ln2_g': 7.839,
     'ln2_b': 8.766}
    for name, (base, spread) in spreads.items():
        noise = np.random.default_rng([zlib.crc32(name.encode()), seed]).standard_normal(out[name].shape)
        drawn = base * np.exp(spread * noise) if base else spread * noise
        out[name] = __import__('jax').numpy.asarray(drawn.astype(out[name].dtype))
    for name, factor in factors.items():
        out[name] = (out[name] * factor).astype(out[name].dtype)
    return out
```

```python
from contextlib import ExitStack

import concourse.bass as bass
from concourse import mybir

F32 = mybir.dt.float32
I32 = mybir.dt.int32
U8 = mybir.dt.uint8
ALU = mybir.AluOpType
ACT = mybir.ActivationFunctionType
AX = mybir.AxisListType

P = 128
D = 1024
KD = D // P
G = 512
C = G // P
SEQ = 128
LAT = 256
T = SEQ + LAT
NT = T // P
SPANS = [(0, SEQ), (SEQ, T)]
H = 4
NE = 16
NG = 4
NPAIR = NE // 2
D_IN = 11 * G + 16
GATE_OFF = 11 * G
ALPHA = 2.0 ** 0.25
EPS = 1e-5
TINY = 1e-30
BIG = 1e30
KSCALE = float(P) ** -0.5
U = C * T
LEVELS = 7
PIECE = 4096
NSLOT = 6

ADA = [n if n < 4 else 11 + n for n in range(12)]
WIN_ORDER = ["rx", "rg", "gq", "gff", "gfb", "gi", "go", "mq", "mk", "mv", "mo"]
WIN_COL = {"rx": 0, "rg": 1, "gq": 2, "gff": 3, "gfb": 4, "gi": 5, "go": 6, "mq": 7, "mk": 8, "mv": 9, "mo": 10}
WIN = {g: 4 + n for n, g in enumerate(WIN_ORDER)}
WOUT = [23, 24, 25]
FIRST_EXPERT = 26

A_BIN, A_ADA, A_CONVW, A_CONVB, A_HGG, A_MLG, A_ROWS = 0, 44, 92, 108, 112, 116, 120
B_BA, B_BX, B_LAM, B_LB, B_H0, B_N0, B_C, B_ROWS = 0, 8, 16, 24, 32, 40, 48, 64
SH1, SC1, G1, SH2, SC2, G2 = range(6)

SEMS = (
    "rows_in x_in pos_in consts_in masks_in masks_cast gate_w_in lru_w_in vbias_in mini_in s0_in c0_in x2_in pos2_in ln_in out_h "
    "out_S out_C out_n out_m out_y z_ready lb_diff lb_exp lam_abs lam_exp z_taken silu_c pos_added cols_ready mod1_ready h_ready "
    "rx_conv sp_ready lru_w_ready lru_zeroed gates_ready gates_taken lru_act lru_den lru_sqrt lru_done vbias_added "
    "dve pool hg_start hg_qk hg_scores hg_taken hg_level hg_final kb_T kb_T_sb s_fin s_fin_sb o_ready o_sq o_var o_std "
    "o_norm gz_ready gz_rows gz_rows_T f_abs f_exp f_ln m_rows c_T c_cols bc_ready p_arg p_exp p_mask kT_ready ke_ready "
    "cfin_ready cfin_sb w_ready si_ready qs_ready num_ready den_floor den_abs h_done hm_ready hc_ready hsq_ready hv_ready "
    "hstd_ready ml_done mod2_ready bcast_ready bcast_taken y_ready ln_var ln_std h2_ready h2_T h2_T_sb logits_ready "
    "smax_ready sexp_ready mask_ready ranks_ready route_ready sel_cols sel_ready gathered gather_taken gate_done up_done "
    "sg_ready act_ready act_T act_T_sb down_done down_sb scattered y_added ln2_var ln2_std out_tile over_shift"
).split()


def z_jobs():
    jobs = [("rows",)] + [("xT", i, half) for i in range(NT) for half in range(2)]

    def ada(first, last):
        out = []
        for n in range(first, last + 1):
            if n < last:
                out.append(("ada_row", n))
            if n > first:
                out.append(("ada_col", n - 1))
        return out

    def group(g):
        if g in ("gi", "mv"):
            return [("tok", g, i) for i in range(NT)]
        return [("chan", g, c) for c in range(C)]

    jobs += ada(0, 4)
    for g in ("rx", "rg", "gq"):
        jobs += group(g)
    jobs += [("lru", 0)] + group("gff")[:1] + [("lru2", 0)] + group("gff")[1:]
    jobs += [("lru", 1)] + group("gfb")[:1] + [("lru2", 1)] + group("gfb")[1:]
    jobs += [("lru", 2)] + group("gi")[:1] + [("lru2", 2)] + group("gi")[1:]
    jobs += [("lru", 3)] + group("go")[:1] + [("lru2", 3)] + group("go")[1:]
    jobs += [("hg_diag",)] + [("gates",)]
    rest = [("hg_level", n) for n in range(LEVELS + 1)]
    proj = [group("mq"), group("mk"), group("mv"), group("mo"), ada(4, 8), ada(8, 12)]
    for n, r in enumerate(rest):
        jobs += proj[n] if n < len(proj) else []
        jobs.append(r)
    return jobs


JOBS = z_jobs()
Z_KINDS = ("rows", "xT", "ada_row", "ada_col", "tok", "chan", "gates")
Z_INDEX = {}
for _job in JOBS:
    if _job[0] in Z_KINDS:
        Z_INDEX[_job] = len(Z_INDEX)


def halves(ap, h):
    v = ap.rearrange("p (b x) -> p b x", x=2 * h)
    return v[:, :, 0:h], v[:, :, h:2 * h]


def build(nc, a, outs):
    with ExitStack() as ctx:
        def sb(name, shape, dt=F32):
            return ctx.enter_context(nc.sbuf_tensor(name, shape, dt))

        S = {n: ctx.enter_context(nc.semaphore(n)) for n in SEMS}
        ring_full = [ctx.enter_context(nc.semaphore(f"ring_full{n}")) for n in range(NSLOT)]

        ring = sb("ring", [P, NSLOT, PIECE])
        arena = sb("arena", [P, 16 * U])
        hT = sb("hT", [P, KD, T])
        small = sb("small", [P, 912])
        ps = ctx.enter_context(nc.psum_tensor("ps", [P, 8, 512], F32))

        at = [0]

        def carve(n):
            at[0] += n
            assert at[0] <= 912
            return small[:, at[0] - n:at[0]]

        def unit(i, off=0, n=U):
            return arena[:, i * U + off:i * U + off + n]

        ident = carve(128)
        ones = carve(128)
        colsA = carve(A_ROWS)
        colsB = carve(B_ROWS)
        modc = carve(96).rearrange("p (v s) -> p v s", s=2)
        sc1p = carve(16).rearrange("p (v s) -> p v s", s=2)
        silu_cols = carve(16)
        h_fin = carve(8).rearrange("p (d c) -> p d c", d=2)
        lb = carve(8)
        om_lb = carve(8)
        neg_om_lb = carve(8)
        psp = carve(8)
        nsp = carve(8)
        tiny_tmp = carve(32)
        eps = carve(1)
        c_cols = carve(24).rearrange("p (d i h) -> p d i h", d=2, i=NT)
        m0_rows = carve(2)
        m0_cols = carve(8)
        m_fin = carve(2)
        n_fin = carve(8)
        gz = carve(48).rearrange("p (i g) -> p i g", i=NT)
        gbias = carve(16)
        mv_stats = carve(14)
        w_router = carve(128).rearrange("p (k e) -> p k e", k=KD)
        rstd = carve(1)

        x_in = arena[:, 8 * U:8 * U + NT * D].rearrange("p (i d) -> p i d", i=NT)
        pos_in = arena[:, 10 * U:10 * U + 2 * D].rearrange("p (i d) -> p i d", i=2)
        ada_early = unit(7, 0, 1024).rearrange("p (b n) -> p b n", b=2)
        ada_late = hT[:, 0:3, :].rearrange("p k t -> p (k t)")[:, 0:1024].rearrange("p (b n) -> p b n", b=2)
        rowsA = unit(0, 0, 128)
        rowsB = unit(0, 128, 128)
        w_bd = arena[:, 11 * U + 512:11 * U + 512 + 16 * P].rearrange("p (d g c e) -> p d g c e", d=2, g=2, c=C)
        RX, XC = unit(0), unit(1)
        R_, I_ = unit(2, 0, 768), unit(2, 768, 768)
        A_ = unit(3, 0, 768)
        LT, HB = unit(0, 0, 768), unit(0, 768, 768)
        zeros4 = unit(3, 1024, 256)
        gate_w = unit(3, 1280, 128).rearrange("p (k g) -> p k g", k=KD)
        mean_w = unit(3, 1408, 128)
        QFF, FF, FB = unit(4), unit(5), unit(6)
        QFB, KBF, KBB = unit(0), unit(1), unit(2)
        VH = unit(7).rearrange("p (i n) -> p i n", i=NT)
        S0 = unit(3, 0, 1024).rearrange("p (x e) -> p x e", x=8)
        SCO = unit(11).rearrange("p (i h t) -> p i h t", i=NT, h=H)
        SCX = unit(12, 0, 1024).rearrange("p (d h t) -> p d h t", d=2, h=H)
        hg_masks = unit(12, 1024, 448).bitcast(U8).rearrange("p (d l t) -> p d l t", d=2, l=LEVELS)
        masks_wide = arena[:, 14 * U:14 * U + 2 * LEVELS * P]
        YR, YH, YM = unit(13), unit(14), unit(15)
        MQ, MK = unit(8), unit(9)
        MV = unit(10).rearrange("p (i n) -> p i n", i=NT)
        S_FIN = unit(6, 0, 1024).rearrange("p (x e) -> p x e", x=8)
        KB_T = unit(5, 1024, 512).rearrange("p (b s) -> p b s", b=4)
        O_SQ = unit(2, 0, 768).rearrange("p (b t) -> p b t", b=2)
        O_STD = unit(1, 0, 768).rearrange("p (b t) -> p b t", b=2)
        hflat = hT[:, :, :].rearrange("p k t -> p (k t)")
        GI = hflat[0:H, 1024:1792].rearrange("p (d t) -> p d t", d=2)
        GF = hflat[0:H, 1792:2560].rearrange("p (d t) -> p d t", d=2)
        BR = unit(1)[0:H, 0:768].rearrange("p (d t) -> p d t", d=2)
        CR = unit(1)[0:H, 768:1536].rearrange("p (d t) -> p d t", d=2)
        MR = unit(0)[0:H, 0:768].rearrange("p (d t) -> p d t", d=2)
        NBM = unit(0)[0:H, 768:1536].rearrange("p (d t) -> p d t", d=2)
        FE = unit(2)[0:H, 0:768].rearrange("p (d t) -> p d t", d=2)
        C0 = unit(5, 0, 1024).rearrange("p (x e) -> p x e", x=8)
        PW_ = unit(11, 0, 1024).rearrange("p (b x) -> p b x", b=2)
        WW = arena[:, 11 * U + 1024:11 * U + 2048].rearrange("p (b x) -> p b x", b=2)
        QS = unit(3, 0, 512).rearrange("p (b x) -> p b x", b=2)
        SI = unit(3, 512, 512).rearrange("p (b x) -> p b x", b=2)
        FLOOR = unit(2, 0, 768).rearrange("p (b x) -> p b x", b=2)
        DEN = unit(2, 768, 768).rearrange("p (b x) -> p b x", b=2)
        HS = unit(4, 0, 768).rearrange("p (b x) -> p b x", b=2)
        HT2 = unit(4, 768, 768).rearrange("p (b x) -> p b x", b=2)
        KE = unit(5, 1024, 256).rearrange("p (b x) -> p b x", b=2)
        C_FIN = unit(7, 0, 1024).rearrange("p (x e) -> p x e", x=8)

        def moe(off, n):
            return arena[:, off:off + n]

        X1 = moe(0, 3072).rearrange("p (i d) -> p i d", i=NT)
        H2 = moe(3072, 3072).rearrange("p (i d) -> p i d", i=NT)
        g1_b = moe(6144, 2048).rearrange("p (s d) -> p s d", s=2)
        sc2_b = moe(8192, 2048).rearrange("p (s d) -> p s d", s=2)
        sh2_b = moe(10240, 2048).rearrange("p (s d) -> p s d", s=2)
        g2_b = moe(12288, 2048).rearrange("p (s d) -> p s d", s=2)
        ln_b = moe(14336, 4096).rearrange("p (v d) -> p v d", v=4)
        pos2 = moe(3072 + 1024, 2048).rearrange("p (i d) -> p i d", i=2)
        h2T = hT
        YACC = moe(19968, 3072).rearrange("p (i d) -> p i d", i=NT)

        def tok16(n):
            return moe(18432 + 48 * n, 48).rearrange("p (i e) -> p i e", i=NT)

        scores, sel, masked, oh1, oh2, mask, comb, t16a, t16b, ranks, posm = [tok16(n) for n in range(11)]
        g12 = [moe(18960 + 12 * n, 12).rearrange("p (i g) -> p i g", i=NT) for n in range(8)]
        r3 = [moe(19056 + 3 * n, 3) for n in range(6)]
        PW = moe(19074, 96).rearrange("p (e i w) -> p e i w", e=NE, i=NT)
        b_router = moe(19170, 16)
        over_f = moe(19186, 2)
        over_i = moe(19188, 2).bitcast(I32)
        pw = moe(19190, 6).rearrange("p (i w) -> p i w", i=NT)
        desc16 = moe(19200, 16)
        tri = moe(19216, 128)
        iota = moe(19344, 128)
        Sel = moe(6144, 384).rearrange("p (i j) -> p i j", i=NT)
        SelW = moe(6528, 384).rearrange("p (i j) -> p i j", i=NT)
        SelWT = moe(6912, 768).rearrange("p (b t) -> p b t", b=2)
        hgT = moe(7680, 1024).rearrange("p (k j) -> p k j", k=KD)
        SG = moe(8704, 512)
        AC = moe(9216, 512)
        ACT_T = moe(9728, 512).rearrange("p (k j) -> p k j", k=C)
        DN = moe(10240, 1024)

        def chunk(ap, c):
            return ap[:, c * T:(c + 1) * T]

        block = ctx.enter_context(nc.Block())

        @block.sync
        def _(sp):
            win_v = a["w_in"][0].rearrange("(k p) n -> p k n", p=P)
            ada_v = a["w_ada"][0].rearrange("(k p) n -> p k n", p=P)

            def rows(dst, at_, src, n):
                sp.dma_start(dst[at_:at_ + n, :], src).then_inc(S["rows_in"], 16)

            flat = "(c p) -> c p"
            rows(rowsA, A_BIN, a["b_in"][0, 0:GATE_OFF].rearrange(flat, p=P), 44)
            rows(rowsA, A_ADA, a["b_ada"][0].rearrange(flat, p=P), 48)
            rows(rowsA, A_CONVW, a["conv_w"][0].rearrange("w (c p) -> (w c) p", p=P), 16)
            rows(rowsA, A_CONVB, a["conv_b"][0].rearrange(flat, p=P), 4)
            rows(rowsA, A_HGG, a["hg_norm_g"][0].rearrange(flat, p=P), 4)
            rows(rowsA, A_MLG, a["ml_norm_g"][0].rearrange(flat, p=P), 4)
            for off, name in ((B_BA, "lru_ba"), (B_BX, "lru_bx"), (B_LAM, "lru_lam"), (B_LB, "hg_lb"), (B_H0, "state_lru_h")):
                src = a[name][0, 0] if name == "state_lru_h" else a[name][0]
                rows(rowsB, off, src.rearrange("d (c p) -> (d c) p", p=P), 8)
            rows(rowsB, B_N0, a["state_mlstm_n"][0, 0].rearrange("d h p -> (d h) p"), 8)
            rows(rowsB, B_C, a["c_ctx"].rearrange(flat, p=P), 8)
            rows(rowsB, B_C + 8, a["c"][0].rearrange(flat, p=P), 8)

            last_job = {ADA[n]: ("ada_row", n) for n in range(12)}
            last_job.update({WIN[g]: ("tok", g, NT - 1) if g in ("gi", "mv") else ("chan", g, C - 1) for g in WIN})

            def piece(n, src, k):
                if n >= NSLOT:
                    if n - NSLOT in last_job:
                        sp.wait_ge(S["z_ready"], Z_INDEX[last_job[n - NSLOT]] + 1)
                    else:
                        sp.wait_ge(S["y_ready"], 2 * NT)
                sp.dma_start(ring[:, n % NSLOT, :].rearrange("p (k n) -> p k n", k=k), src).then_inc(ring_full[n % NSLOT], 16)

            for n in range(4):
                piece(n, ada_v[:, :, n * G:(n + 1) * G], KD)
            for g in WIN_ORDER:
                piece(WIN[g], win_v[:, :, WIN_COL[g] * G:(WIN_COL[g] + 1) * G], KD)
            for n in range(4, 12):
                piece(ADA[n], ada_v[:, :, n * G:(n + 1) * G], KD)
            for n in range(3):
                piece(WOUT[n], a["w_out"][0, n * G:(n + 1) * G, :].rearrange("(k p) n -> p k n", p=P), C)
            names = ("w_gate", "w_up", "w_down")
            for n in range(6):
                piece(FIRST_EXPERT + n, a[names[n % 3]][0, n // 3].rearrange("(k p) n -> p k n", p=P), C if n % 3 == 2 else KD)

            def expert_pairs(first, start):
                with sp.Fori(start, NPAIR) as i:
                    for e in range(2):
                        for j in range(3):
                            slot = (FIRST_EXPERT + 3 * e + j) % NSLOT
                            sp.wait_ge(S[("gate_done", "up_done", "down_done")[j]], 2 * i + (first + e - 1))
                            src = a[names[j]][0].rearrange("(i e) d f -> i e d f", e=2)[bass.ds(i, 1), e]
                            src = src.rearrange("a (k p) n -> p (a k) n", p=P)
                            k = C if j == 2 else KD
                            sp.dma_start(ring[:, slot, :].rearrange("p (k n) -> p k n", k=k), src).then_inc(ring_full[slot], 16)

            expert_pairs(0, 1)
            sp.wait_ge(S["route_ready"], 1)
            over = sp.value_load(over_i[0:1, 0:1], min_val=0, max_val=T)
            with sp.If(over > P):
                expert_pairs(NE, 0)
                expert_pairs(2 * NE, 0)

        @block.gpsimd
        def _(pool):
            pool.dma_start(ident, a["consts"][:, 0:128]).then_inc(S["consts_in"], 16)
            pool.dma_start(x_in[:, 0, :], a["x_prompt"][0]).then_inc(S["x_in"], 16)
            pool.dma_start(x_in[:, 1:3, :], a["x_sample"][0].rearrange("(i p) d -> p i d", p=P)).then_inc(S["x_in"], 16)
            pool.dma_start(pos_in, a["pos"].rearrange("(i p) d -> p i d", p=P)).then_inc(S["pos_in"], 16)
            pool.dma_start(gate_w, a["w_in"][0, :, GATE_OFF:D_IN].rearrange("(k p) n -> p k n", p=P)).then_inc(S["gate_w_in"], 16)
            pool.dma_start(gbias, a["b_in"][0, GATE_OFF:D_IN].partition_broadcast(P)).then_inc(S["gate_w_in"], 16)
            pool.dma_start(w_router, a["w_router"].rearrange("(k p) n -> p k n", p=P)).then_inc(S["mini_in"], 16)
            pool.dma_start(m0_rows[0:H, :], a["state_mlstm_m"][0, 0].rearrange("d h -> h d"), allow_slow_non_contiguous=True).then_inc(S["mini_in"], 16)
            pool.dma_start(m0_cols, a["state_mlstm_m"][0, 0].rearrange("d h -> (d h)").partition_broadcast(P)).then_inc(S["mini_in"], 16)
            pool.dma_start(masks_wide, a["hg_masks"]).then_inc(S["masks_in"], 16)
            pool.wait_ge(S["masks_in"], 16)
            pool.tensor_copy(hg_masks.rearrange("p d l t -> p (d l t)"), masks_wide).then_inc(S["masks_cast"], 1)
            pool.wait_ge(S["z_taken"], 7)
            pool.memset(w_bd, 0.0).then_inc(S["lru_zeroed"], 1)
            pool.wait_ge(S["lru_zeroed"], 1)
            for d in range(2):
                for g, name in enumerate(("lru_wa", "lru_wx")):
                    for b in range(2):
                        src = a[name][0, d].rearrange("(c b) i e -> b i c e", b=2)[b]
                        pool.dma_start(w_bd[64 * b:64 * b + 64, d, g, :, 64 * b:64 * b + 64], src).then_inc(S["lru_w_in"], 16)

            def value_bias(n, g, dst, row):
                pool.dma_start(row, a["b_in"][0, WIN_COL[g] * G:(WIN_COL[g] + 1) * G].partition_broadcast(P)).then_inc(S["vbias_in"], 16)
                pool.wait_ge(S["vbias_in"], 16 * (n + 1))
                for i in range(NT):
                    pool.wait_ge(S["z_taken"], Z_INDEX[("tok", g, i)] + 1)
                    pool.tensor_tensor(dst[:, i, :], dst[:, i, :], row, ALU.add).then_inc(S["vbias_added"], 1)

            pool.wait_ge(S["pos_added"], 1)
            value_bias(0, "gi", VH, unit(10, 0, G))
            pool.wait_ge(S["lru_done"], C)
            pool.dma_start(S0, a["state_hgrn_S"][0, 0].rearrange("d h p e -> p (d h) e")).then_inc(S["s0_in"], 16)
            pool.wait_ge(S["hg_final"], 1)
            pool.dma_start(C0, a["state_mlstm_C"][0, 0].rearrange("d h p e -> p (d h) e")).then_inc(S["c0_in"], 16)
            pool.wait_ge(S["z_taken"], len(Z_INDEX))
            value_bias(1, "mv", MV, hflat[:, 2560:3072])
            pool.dma_start(outs[2][0, 0].rearrange("d (c p) -> p d c", p=P), h_fin, allow_slow_non_contiguous=True).then_inc(S["out_h"], 16)
            pool.wait_ge(S["s_fin_sb"], 8)
            pool.dma_start(outs[3][0, 0].rearrange("d h p e -> p (d h) e"), S_FIN).then_inc(S["out_S"], 16)
            pool.wait_ge(S["m_rows"], 1)
            pool.dma_start(outs[6][0, 0].rearrange("d h -> h d"), m_fin[0:H, :], allow_slow_non_contiguous=True).then_inc(S["out_m"], 16)
            for n in range(8):
                d = n % 2
                pool.wait_ge(S["p_exp"], n + 1)
                pool.wait_ge(S["ke_ready"], n + 1)
                v = PW_[:, n % 2, :].rearrange("p (b t) -> p b t", t=P)
                sgn = 1 - 2 * d
                for part, nb in ((v[:, 0:2, :], 2), (v[:, 3:4, :], 1)):
                    ins = pool.affine_select(out=part, in_=part, compare_op=ALU.is_ge, fill=0.0, base=0,
                                             pattern=[[0, nb], [sgn, P]], channel_multiplier=-sgn)
                    ins.then_inc(S["p_mask"], 1)
            pool.wait_ge(S["cfin_sb"], 8)
            pool.dma_start(outs[4][0, 0].rearrange("d h p e -> p (d h) e"), C_FIN).then_inc(S["out_C"], 16)
            pool.dma_start(outs[5][0, 0].rearrange("d h p -> p (d h)"), n_fin, allow_slow_non_contiguous=True).then_inc(S["out_n"], 16)
            pool.wait_ge(S["ml_done"], 1)
            pool.dma_start(X1[:, 0, :], a["x_prompt"][0]).then_inc(S["x2_in"], 16)
            pool.dma_start(X1[:, 1:3, :], a["x_sample"][0].rearrange("(i p) d -> p i d", p=P)).then_inc(S["x2_in"], 16)
            pool.dma_start(pos2, a["pos"].rearrange("(i p) d -> p i d", p=P)).then_inc(S["pos2_in"], 16)
            for v, name in enumerate(("ln1_g", "ln1_b", "ln2_g", "ln2_b")):
                pool.dma_start(ln_b[:, v, :], a[name][0].partition_broadcast(P)).then_inc(S["ln_in"], 16)
            pool.dma_start(b_router, a["b_router"].partition_broadcast(P)).then_inc(S["ln_in"], 16)
            pool.dma_start(tri, a["consts"][:, 128:256]).then_inc(S["ln_in"], 16)
            pool.dma_start(iota, a["consts"][:, 256:384]).then_inc(S["ln_in"], 16)
            pool.dma_start(desc16, a["consts"][:, 384:400]).then_inc(S["ln_in"], 16)
            for i in range(NT):
                pool.wait_ge(S["out_tile"], i + 1)
                dst = outs[0][0] if i == 0 else outs[1][0, (i - 1) * P:i * P, :]
                pool.dma_start(dst, X1[:, i, :]).then_inc(S["out_y"], 16)
            pool.wait_ge(S["out_y"], 16 * NT)
            for n in ("out_h", "out_S", "out_C", "out_n", "out_m"):
                pool.wait_ge(S[n], 16)

        @block.scalar
        def _(act):
            done = {}

            def step(ins, name):
                done[name] = done.get(name, 0) + 1
                ins.then_inc(S[name], 1)
                act.wait_ge(S[name], done[name])

            bias_col = {g: A_BIN + 4 * WIN_COL[g] for g in WIN_COL}
            func = {"rx": ACT.Identity, "rg": ACT.Gelu_apprx_tanh, "gq": ACT.Silu, "gff": ACT.Sigmoid, "gfb": ACT.Sigmoid,
                    "go": ACT.Silu, "mq": ACT.Identity, "mk": ACT.Identity, "mo": ACT.Sigmoid}
            dst_of = {"rx": RX, "rg": YR, "gq": QFF, "gff": FF, "gfb": FB, "go": YH, "mq": MQ, "mk": MK, "mo": YM}

            def lru_gates(c):
                act.wait_ge(S["gates_ready"], c + 1)
                act.wait_ge(S["sp_ready"], 1)
                if c:
                    act.wait_ge(S["lru_done"], c)
                for d in range(2):
                    act.activation(R_[:, d * T:(d + 1) * T], ps[:, 4 + 2 * d, 0:T], ACT.Sigmoid,
                                   bias=colsB[:, B_BA + 4 * d + c:B_BA + 4 * d + c + 1]).then_inc(S["gates_taken"], 1)
                    act.activation(I_[:, d * T:(d + 1) * T], ps[:, 5 + 2 * d, 0:T], ACT.Sigmoid,
                                   bias=colsB[:, B_BX + 4 * d + c:B_BX + 4 * d + c + 1]).then_inc(S["gates_taken"], 1)
                act.wait_ge(S["gates_taken"], 4 * c + 4)
                for d in range(2):
                    k = 4 * d + c
                    step(act.activation(A_[:, d * T:(d + 1) * T], R_[:, d * T:(d + 1) * T], ACT.Exp, scale=nsp[:, k:k + 1]), "lru_act")
                for d in range(2):
                    k = 4 * d + c
                    step(act.activation(R_[:, d * T:(d + 1) * T], R_[:, d * T:(d + 1) * T], ACT.Tanh, scale=psp[:, k:k + 1]), "lru_act")

            def lru_sqrt(c):
                act.wait_ge(S["lru_den"], c + 1)
                act.activation(R_, R_, ACT.Sqrt, scale=2.0).then_inc(S["lru_sqrt"], 1)

            for job in JOBS:
                kind = job[0]
                if kind == "lru":
                    lru_gates(job[1])
                    continue
                if kind == "lru2":
                    lru_sqrt(job[1])
                    continue
                if kind not in Z_KINDS:
                    continue
                n = Z_INDEX[job]
                bank = ps[:, n % 4, :]
                act.wait_ge(S["z_ready"], n + 1)
                if kind == "rows":
                    act.activation(colsA, bank[:, 0:A_ROWS], ACT.Identity).then_inc(S["cols_ready"], 1)
                    act.activation(colsB, bank[:, 128:128 + B_ROWS], ACT.Identity).then_inc(S["cols_ready"], 1)
                    act.wait_ge(S["cols_ready"], 2)
                    act.activation(silu_cols, colsB[:, B_C:B_C + 16], ACT.Silu).then_inc(S["z_taken"], 1)
                elif kind == "xT":
                    _, i, half = job
                    act.activation(hT[:, 4 * half:4 * half + 4, i * P:(i + 1) * P], bank.rearrange("p (k t) -> p k t", k=4),
                                   ACT.Identity).then_inc(S["z_taken"], 1)
                    if (i, half) == (NT - 1, 1):
                        act.wait_ge(S["lb_diff"], 1)
                        act.activation(tiny_tmp[:, 0:8], tiny_tmp[:, 0:8], ACT.Exp).then_inc(S["lb_exp"], 1)
                        act.wait_ge(S["lam_abs"], 1)
                        act.activation(nsp, nsp, ACT.Exp, scale=-1.0).then_inc(S["lam_exp"], 1)
                elif kind == "ada_row":
                    buf = ada_early if job[1] < 4 else ada_late
                    act.activation(buf[0:2, job[1] % 2, :], bank[0:2, :], ACT.Identity).then_inc(S["z_taken"], 1)
                elif kind == "ada_col":
                    act.activation(modc[:, 4 * job[1]:4 * job[1] + 4, :], bank[:, 0:8].rearrange("p (c s) -> p c s", s=2),
                                   ACT.Identity).then_inc(S["z_taken"], 1)
                elif kind == "tok":
                    _, g, i = job
                    if g == "mv" and i == 0:
                        act.wait_ge(S["vbias_added"], NT)
                    act.activation((VH if g == "gi" else MV)[:, i, :], bank, ACT.Identity).then_inc(S["z_taken"], 1)
                elif kind == "gates":
                    act.activation(gz, bank[:, 0:48].rearrange("p (i g) -> p i g", i=NT), ACT.Identity).then_inc(S["z_taken"], 1)
                else:
                    _, g, c = job
                    bias = colsA[:, bias_col[g] + c:bias_col[g] + c + 1]
                    if g == "go" and c == 0:
                        act.wait_ge(S["masks_cast"], 1)
                    if g == "mk":
                        act.wait_ge(S["sp_ready"], 1)
                        act.activation(chunk(MK, c), bank[:, 0:T], ACT.Identity, bias=tiny_tmp[:, 28 + c:29 + c], scale=KSCALE).then_inc(S["z_taken"], 1)
                    else:
                        act.activation(chunk(dst_of[g], c), bank[:, 0:T], func[g], bias=bias).then_inc(S["z_taken"], 1)

            for n in range(8):
                act.wait_ge(S["kb_T"], n + 1)
                if n == 0:
                    act.wait_ge(S["hg_final"], 1)
                if n >= 4:
                    act.wait_ge(S["s_fin"], n - 3)
                act.activation(KB_T[:, n % 4, :], ps[:, n % 2, 0:P], ACT.Identity).then_inc(S["kb_T_sb"], 1)
                if n >= 1:
                    act.wait_ge(S["s_fin"], n)
                    act.activation(S_FIN[:, n - 1, :], ps[:, 2 + (n - 1) % 2, 0:P], ACT.Identity).then_inc(S["s_fin_sb"], 1)
            act.wait_ge(S["s_fin"], 8)
            act.activation(S_FIN[:, 7, :], ps[:, 3, 0:P], ACT.Identity).then_inc(S["s_fin_sb"], 1)
            for h in range(H + 1):
                if h < H:
                    act.wait_ge(S["o_ready"], h + 1)
                    if h >= 2:
                        act.wait_ge(S["o_var"], h - 1)
                    act.activation(O_SQ[:, h % 2, :], ps[:, 4 + h % 2, 0:T], ACT.Square).then_inc(S["o_sq"], 1)
                if h >= 1:
                    act.wait_ge(S["o_var"], h)
                    if h >= 3:
                        act.wait_ge(S["o_norm"], h - 2)
                    act.activation(O_STD[:, (h - 1) % 2, :], ps[:, 6 + (h - 1) % 2, 0:T], ACT.Sqrt, bias=eps).then_inc(S["o_std"], 1)

            for d in range(2):
                act.wait_ge(S["gz_rows_T"], 2 * d + 1)
                act.activation(GI[:, d, :], ps[0:H, 2 * d, 0:T], ACT.Identity).then_inc(S["gz_rows"], 1)
                act.wait_ge(S["gz_rows_T"], 2 * d + 2)
                act.activation(GF[:, d, :], ps[0:H, 2 * d + 1, 0:T], ACT.Identity).then_inc(S["gz_rows"], 1)
            act.wait_ge(S["f_abs"], 1)
            act.activation(FE, FE, ACT.Exp, scale=-1.0).then_inc(S["f_exp"], 1)
            act.wait_ge(S["f_exp"], 1)
            act.activation(FE, FE, ACT.Ln, bias=1.0).then_inc(S["f_ln"], 1)
            act.wait_ge(S["c_T"], 1)
            act.activation(c_cols.rearrange("p d i h -> p (d i h)"), ps[:, 0, 0:24], ACT.Identity).then_inc(S["c_cols"], 1)

            for n in range(8):
                h, d = n // 2, n % 2
                b = n % 2
                act.wait_ge(S["bc_ready"], n + 1)
                if n >= 2:
                    act.wait_ge(S["qs_ready"], n - 1)
                    act.wait_ge(S["h_done"], n - 1)
                act.activation(SI[:, b, :], ps[:, 0, SEQ:T], ACT.Exp, scale=-1.0,
                               bias=m0_cols[:, 4 * d + h:4 * d + h + 1]).then_inc(S["si_ready"], 1)
                act.activation(FLOOR[:, b, :], ps[:, 1, 0:T], ACT.Exp).then_inc(S["den_floor"], 1)
                act.wait_ge(S["p_arg"], n + 1)
                act.activation(PW_[:, b, :], PW_[:, b, :], ACT.Exp, scale=-1.0).then_inc(S["p_exp"], 1)
                act.wait_ge(S["cfin_ready"], n + 1)
                act.activation(C_FIN[:, 4 * d + h, :], ps[:, 3, 0:P], ACT.Identity).then_inc(S["den_floor"], 1)
                act.activation(n_fin[:, 4 * d + h:4 * d + h + 1], ps[:, 3, 128:129], ACT.Identity).then_inc(S["cfin_sb"], 1)
                act.wait_ge(S["num_ready"], n + 1)
                act.activation(DEN[:, b, :], ps[:, 5, 0:T], ACT.Abs).then_inc(S["den_abs"], 1)
                if d == 1:
                    act.wait_ge(S["hc_ready"], h + 1)
                    act.activation(HT2[:, 0, :], HS[:, 0, :], ACT.Square).then_inc(S["hsq_ready"], 1)
                    act.wait_ge(S["hv_ready"], h + 1)
                    act.activation(HT2[:, 1, :], ps[:, 7, 0:T], ACT.Sqrt, bias=eps).then_inc(S["hstd_ready"], 1)

            act.wait_ge(S["ml_done"], 1)
            act.wait_ge(S["out_C"], 16)
            act.wait_ge(S["out_S"], 16)
            for n in range(16):
                v, s, half = n // 4, (n // 2) % 2, n % 2
                dst = (g1_b, sh2_b, sc2_b, g2_b)[v][:, s, half * 512:(half + 1) * 512]
                act.wait_ge(S["bcast_ready"], n + 1)
                act.activation(dst, ps[:, 6 + n % 2, :], ACT.Identity, bias=1.0 if v == 2 else 0.0).then_inc(S["bcast_taken"], 1)

            for i in range(NT):
                act.wait_ge(S["ln_var"], i + 1)
                act.activation(rstd, mv_stats[:, 13:14], ACT.Sqrt, bias=eps).then_inc(S["ln_std"], 1)
                for half in range(2):
                    act.wait_ge(S["h2_T"], 2 * i + half + 1)
                    act.activation(h2T[:, 4 * half:4 * half + 4, i * P:(i + 1) * P], ps[:, 6 + half, :].rearrange("p (k t) -> p k t", k=4),
                                   ACT.Identity).then_inc(S["h2_T_sb"], 1)
            act.wait_ge(S["smax_ready"], 1)
            act.activation(scores, scores, ACT.Exp).then_inc(S["sexp_ready"], 1)

            def gather_out(n, b):
                act.wait_ge(S["gathered"], n + 1)
                for half in range(2):
                    act.activation(hgT[:, 4 * half:4 * half + 4, :], ps[:, half, :].rearrange("p (k j) -> p k j", k=4),
                                   ACT.Identity).then_inc(S["gather_taken"], 1)
                act.activation(SelWT[:, b, :], ps[:, 2, 0:T], ACT.Identity).then_inc(S["gather_taken"], 1)

            def expert(n, b, more):
                act.wait_ge(S["up_done"], n + 1)
                act.activation(SG, ps[:, 3, :], ACT.Silu).then_inc(S["sg_ready"], 1)
                act.wait_ge(S["act_T"], n + 1)
                act.activation(ACT_T, ps[:, 3, :].rearrange("p (k j) -> p k j", k=C), ACT.Identity).then_inc(S["act_T_sb"], 1)
                if more:
                    gather_out(n + 1, 1 - b)
                act.wait_ge(S["down_done"], n + 1)
                for half in range(2):
                    act.activation(DN[:, half * 512:(half + 1) * 512], ps[:, 5 + half, :], ACT.Identity).then_inc(S["down_sb"], 1)

            def expert_pass(base):
                gather_out(base, 0)
                expert(base, 0, True)
                with act.Fori(0, NPAIR - 1) as i:
                    expert(2 * i + (base + 1), 1, True)
                    expert(2 * i + (base + 2), 0, True)
                expert(base + NE - 1, 1, False)

            act.wait_ge(S["route_ready"], 1)
            expert_pass(0)
            over = act.value_load(over_i[0:1, 0:1], min_val=0, max_val=T)
            with act.If(over > P):
                expert_pass(NE)
                expert_pass(2 * NE)
            for i in range(NT):
                act.wait_ge(S["ln2_var"], i + 1)
                act.activation(rstd, mv_stats[:, 13:14], ACT.Sqrt, bias=eps).then_inc(S["ln2_std"], 1)

        @block.tensor
        def _(pe):
            def mm(out, lhsT, rhs, start=True, stop=True, open_=False):
                return pe.matmul(out, lhsT, rhs, start=start, stop=stop, skip_group_check=open_)

            def slot(n, k):
                return ring[:, n % NSLOT, :].rearrange("p (k n) -> p k n", k=k)

            def full(n):
                pe.wait_ge(ring_full[n % NSLOT], 16 * (n // NSLOT + 1))

            def lru(c):
                if c == 0:
                    pe.wait_ge(S["lru_w_in"], 16 * 8)
                    pe.wait_ge(S["rx_conv"], 1)
                else:
                    pe.wait_ge(S["gates_taken"], 4 * c)
                for d in range(2):
                    for g in range(2):
                        last = mm(ps[:, 4 + 2 * d + g, 0:T], w_bd[:, d, g, c, :], chunk(XC, c))
                last.then_inc(S["gates_ready"], 1)

            hg_job = [0]

            def hg_bank():
                m = hg_job[0]
                hg_job[0] += 1
                if m >= 4:
                    pe.wait_ge(S["hg_taken"], m - 3)
                return ps[:, 4 + m % 4, :].rearrange("p (h t) -> p h t", h=H)

            def hg_mul(out, k, q, s, t, start=True, stop=True):
                return mm(out, k[:, s:s + P], q[:, t:t + P], start, stop)

            def hg_diag():
                pe.wait_ge(S["gates_taken"], 4 * C)
                pe.wait_ge(S["hg_start"], 1)
                for i in range(NT):
                    out = hg_bank()
                    for h in range(H):
                        hg_mul(out[:, h, :], chunk(KBF, h), chunk(QFF, h), i * P, i * P, True, False)
                        last = hg_mul(out[:, h, :], chunk(KBB, h), chunk(QFF, h), i * P, i * P, False, True)
                    last.then_inc(S["hg_scores"], 1)

            def hg_level(lv):
                pe.wait_ge(S["hg_level"], lv + 1)
                if lv < LEVELS:
                    todo = [(d, i * P, i * P) for i in range(NT) for d in range(2)]
                else:
                    todo = [(0, P, 2 * P), (1, 2 * P, P)]
                for d, s, t in todo:
                    out = hg_bank()
                    for h in range(H):
                        last = hg_mul(out[:, h, :], chunk((KBF, KBB)[d], h), chunk((QFF, QFB)[d], h), s, t)
                    last.then_inc(S["hg_scores"], 1)

            for job in JOBS:
                kind = job[0]
                if kind == "lru":
                    lru(job[1])
                    continue
                if kind == "hg_diag":
                    hg_diag()
                    continue
                if kind == "hg_level":
                    hg_level(job[1])
                    continue
                if kind not in Z_KINDS:
                    continue
                n = Z_INDEX[job]
                bank = ps[:, n % 4, :]
                if n >= 4:
                    pe.wait_ge(S["z_taken"], n - 3)
                if kind == "rows":
                    pe.wait_ge(S["consts_in"], 16)
                    pe.wait_ge(S["rows_in"], 16 * 14)
                    pe.transpose(bank[:, 0:A_ROWS], rowsA[0:A_ROWS, :], ident[0:A_ROWS, 0:A_ROWS])
                    last = pe.transpose(bank[:, 128:128 + B_ROWS], rowsB[0:B_ROWS, :], ident[0:B_ROWS, 0:B_ROWS])
                elif kind == "xT":
                    _, i, half = job
                    if i == 0 and half == 0:
                        pe.wait_ge(S["x_in"], 32)
                    if i == 1 and half == 0:
                        pe.wait_ge(S["pos_added"], 1)
                    for k in range(4):
                        last = pe.transpose(bank[:, k * P:(k + 1) * P], x_in[:, i, (4 * half + k) * P:(4 * half + k + 1) * P], ident)
                elif kind == "ada_row":
                    full(ADA[job[1]])
                    pe.wait_ge(S["z_taken"], 1)
                    w = slot(ADA[job[1]], KD)
                    for k in range(KD):
                        last = mm(bank[0:2, :], silu_cols[:, k:k + 9:8], w[:, k, :], k == 0, k == KD - 1)
                elif kind == "ada_col":
                    buf = ada_early if job[1] < 4 else ada_late
                    pe.wait_ge(S["z_taken"], Z_INDEX[("ada_row", job[1])] + 1)
                    for c in range(4):
                        last = mm(bank[:, 2 * c:2 * c + 2], buf[0:2, job[1] % 2, c * P:(c + 1) * P], ident[0:2, 0:2])
                elif kind == "tok":
                    _, g, i = job
                    full(WIN[g])
                    w = slot(WIN[g], KD)
                    for k in range(KD):
                        last = mm(bank, hT[:, k, i * P:(i + 1) * P], w[:, k, :], k == 0, k == KD - 1)
                elif kind == "gates":
                    pe.wait_ge(S["gate_w_in"], 32)
                    for i in range(NT):
                        for k in range(KD):
                            last = mm(bank[:, 16 * i:16 * i + 16], hT[:, k, i * P:(i + 1) * P], gate_w[:, k, :], k == 0, k == KD - 1)
                else:
                    _, g, c = job
                    full(WIN[g])
                    if g == "rx":
                        pe.wait_ge(S["h_ready"], 16)
                    w = slot(WIN[g], KD)
                    for k in range(KD):
                        last = mm(bank[:, 0:T], w[:, k, c * P:(c + 1) * P], hT[:, k, :], k == 0, k == KD - 1)
                last.then_inc(S["z_ready"], 1)

            pe.wait_ge(S["z_taken"], len(Z_INDEX))
            pe.wait_ge(S["vbias_added"], NT)
            for n in range(8):
                d, h = n // 4, n % 4
                if n >= 2:
                    pe.wait_ge(S["kb_T_sb"], n - 1)
                pe.transpose(ps[:, n % 2, 0:P], chunk((KBF, KBB)[d], h)[:, 0:P], ident).then_inc(S["kb_T"], 1)
                pe.wait_ge(S["kb_T_sb"], n + 1)
                if n >= 2:
                    pe.wait_ge(S["s_fin_sb"], n - 1)
                mm(ps[:, 2 + n % 2, 0:P], KB_T[:, n % 4, :], VH[:, 0, h * P:(h + 1) * P]).then_inc(S["s_fin"], 1)
            pe.wait_ge(S["s0_in"], 16)
            pe.wait_ge(S["hg_final"], 1)
            pe.wait_ge(S["hg_taken"], hg_job[0])

            def o_var(h):
                pe.wait_ge(S["o_sq"], h + 1)
                if h >= 2:
                    pe.wait_ge(S["o_std"], h - 1)
                mm(ps[:, 6 + h % 2, 0:T], mean_w, O_SQ[:, h % 2, :]).then_inc(S["o_var"], 1)

            for h in range(H):
                o = ps[:, 4 + h % 2, 0:T]
                if h >= 2:
                    pe.wait_ge(S["o_norm"], h - 1)
                v = [VH[:, i, h * P:(h + 1) * P] for i in range(NT)]
                mm(o[:, 0:P], v[0], SCO[:, 0, h, :])
                mm(o[:, SEQ:T], S0[:, h, :], chunk(QFF, h)[:, SEQ:T], True, False)
                mm(o[:, P:2 * P], v[1], SCO[:, 1, h, :], False, False, True)
                mm(o[:, P:2 * P], v[2], SCX[:, 1, h, :], False, False, True)
                mm(o[:, 2 * P:T], v[2], SCO[:, 2, h, :], False, False, True)
                mm(o[:, 2 * P:T], v[1], SCX[:, 0, h, :], False, False, True)
                mm(o[:, SEQ:T], S0[:, 4 + h, :], chunk(QFB, h)[:, SEQ:T], False, True).then_inc(S["o_ready"], 1)
                if h >= 1:
                    o_var(h - 1)
            o_var(H - 1)

            pe.wait_ge(S["gz_ready"], 1)
            pe.wait_ge(S["s_fin_sb"], 8)
            for d in range(2):
                for ty in range(2):
                    for i in range(NT):
                        last = pe.transpose(ps[0:H, 2 * d + ty, i * P:(i + 1) * P], gz[:, i, 8 * d + 4 * ty:8 * d + 4 * ty + 4], ident)
                    last.then_inc(S["gz_rows_T"], 1)
            pe.wait_ge(S["m_rows"], 1)
            for d in range(2):
                for i in range(NT):
                    o = 12 * d + 4 * i
                    last = pe.transpose(ps[:, 0, o:o + 4], CR[:, d, i * P:(i + 1) * P], ident[0:H, 0:H])
            last.then_inc(S["c_T"], 1)
            pe.wait_ge(S["c_cols"], 1)
            pe.wait_ge(S["c0_in"], 16)
            pe.wait_ge(S["vbias_added"], 2 * NT)
            pe.wait_ge(S["o_norm"], H)

            for n in range(8):
                h, d = n // 2, n % 2
                b = n % 2
                pick = ident[0:H, h:h + 1].broadcast_to([H, P])
                if n >= 1:
                    pe.wait_ge(S["p_arg"], n)
                    pe.wait_ge(S["den_floor"], 2 * n)
                mm(ps[:, 0, 0:T], pick, MR[:, d, :])
                mm(ps[:, 1, 0:T], pick, NBM[:, d, :]).then_inc(S["bc_ready"], 1)
                q, k = chunk(MQ, h), chunk(MK, h)
                if n >= 1:
                    pe.wait_ge(S["w_ready"], n)
                mm(ps[:, 2, 0:P], k[:, 0:P], q[:, 0:P])
                if d == 0:
                    mm(ps[:, 2, P:3 * P], k[:, P:2 * P], q[:, P:T])
                    mm(ps[:, 2, 3 * P:4 * P], k[:, 2 * P:T], q[:, 2 * P:T])
                else:
                    mm(ps[:, 2, P:2 * P], k[:, P:2 * P], q[:, P:2 * P])
                    mm(ps[:, 2, 2 * P:4 * P], k[:, 2 * P:T], q[:, P:T])
                if n >= 1:
                    pe.wait_ge(S["cfin_sb"], n)
                pe.transpose(ps[:, 3, 256:384], k[:, 0:P], ident).then_inc(S["kT_ready"], 1)
                pe.wait_ge(S["ke_ready"], n + 1)
                v = [MV[:, i, h * P:(h + 1) * P] for i in range(NT)]
                mm(ps[:, 3, 0:P], KE[:, b, :], v[0])
                mm(ps[:, 3, 128:129], KE[:, b, :], ones[:, 0:1]).then_inc(S["cfin_ready"], 1)
                pe.wait_ge(S["qs_ready"], n + 1)
                pe.wait_ge(S["w_ready"], n + 1)
                if n >= 1:
                    pe.wait_ge(S["h_done"], n)
                w = WW[:, b, :]
                n0 = colsB[:, B_N0 + 4 * d + h:B_N0 + 4 * d + h + 1].broadcast_to([P, P])
                for bank, c0, vs in ((4, C0[:, 4 * d + h, :], v), (5, n0, [ones] * NT)):
                    o = ps[:, bank, 0:T]
                    mm(o[:, 0:P], vs[0], w[:, 0:P])
                    mm(o[:, SEQ:T], c0, QS[:, b, :], True, False)
                    if d == 0:
                        mm(o[:, 2 * P:T], vs[2], w[:, 3 * P:4 * P], False, False, True)
                        last = mm(o[:, SEQ:T], vs[1], w[:, P:3 * P], False, True)
                    else:
                        mm(o[:, P:2 * P], vs[1], w[:, P:2 * P], False, False, True)
                        last = mm(o[:, SEQ:T], vs[2], w[:, 2 * P:4 * P], False, True)
                last.then_inc(S["num_ready"], 1)
                if d == 1:
                    pe.wait_ge(S["h_done"], n + 1)
                    mm(ps[:, 6, 0:T], mean_w, HS[:, 1, :]).then_inc(S["hm_ready"], 1)
                    pe.wait_ge(S["hsq_ready"], h + 1)
                    mm(ps[:, 7, 0:T], mean_w, HT2[:, 0, :]).then_inc(S["hv_ready"], 1)

            pe.wait_ge(S["mod2_ready"], 1)
            pe.wait_ge(S["ml_done"], 1)
            for n in range(16):
                v, s, half = n // 4, (n // 2) % 2, n % 2
                if n >= 2:
                    pe.wait_ge(S["bcast_taken"], n - 1)
                for k in range(4):
                    col = modc[:, 8 * (G1, SH2, SC2, G2)[v] + 4 * half + k, s:s + 1].broadcast_to([P, P])
                    last = mm(ps[:, 6 + n % 2, k * P:(k + 1) * P], col, ident)
                last.then_inc(S["bcast_ready"], 1)

            for n in WOUT:
                full(n)
            for i in range(NT):
                for half in range(2):
                    for kk in range(12):
                        y = (YR, YH, YM)[kk // 4]
                        last = mm(ps[:, 2 * i + half, :], chunk(y, kk % 4)[:, i * P:(i + 1) * P],
                                  slot(WOUT[kk // 4], C)[:, kk % 4, half * 512:(half + 1) * 512], kk == 0, kk == 11)
                    last.then_inc(S["y_ready"], 1)

            pe.wait_ge(S["bcast_taken"], 16)
            pe.wait_ge(S["mini_in"], 48)
            for i in range(NT):
                pe.wait_ge(S["h2_ready"], i + 1)
                for half in range(2):
                    if i:
                        pe.wait_ge(S["h2_T_sb"], 2 * i - 1 + half)
                    for k in range(4):
                        last = pe.transpose(ps[:, 6 + half, k * P:(k + 1) * P], H2[:, i, (4 * half + k) * P:(4 * half + k + 1) * P], ident)
                    last.then_inc(S["h2_T"], 1)
                pe.wait_ge(S["h2_T_sb"], 2 * i + 2)
                for k in range(KD):
                    last = mm(ps[:, 0, 16 * i:16 * i + 16], h2T[:, k, i * P:(i + 1) * P], w_router[:, k, :], k == 0, k == KD - 1)
            last.then_inc(S["logits_ready"], 1)
            pe.wait_ge(S["mask_ready"], 1)
            pe.wait_ge(S["ln_in"], 16 * 8)
            for i in range(NT):
                for j in range(i + 1):
                    mm(ps[:, 1, 16 * i:16 * i + 16], tri if j == i else ones, mask[:, j, :], j == 0, j == i)
            for j in range(NT):
                last = mm(ps[:, 1, 48:64], ones, mask[:, j, :], j == 0, j == NT - 1)
            last.then_inc(S["ranks_ready"], 1)

            def gather(n, wait_y=True):
                pe.wait_ge(S["sel_ready"], n + 1)
                if wait_y:
                    pe.wait_ge(S["y_added"], 6 * n - 6)
                for k in range(KD):
                    for i in range(NT):
                        mm(ps[:, k // 4, (k % 4) * P:(k % 4 + 1) * P], H2[:, i, k * P:(k + 1) * P], Sel[:, i, :], i == 0, i == NT - 1)
                for i in range(NT):
                    last = pe.transpose(ps[:, 2, i * P:(i + 1) * P], SelW[:, i, :], ident)
                last.then_inc(S["gathered"], 1)

            def gate_up(n, m, pair):
                pe.wait_ge(S["gather_taken"], 3 * n + 3)
                for j, bank in ((0, 3), (1, 4)):
                    p0 = FIRST_EXPERT + 3 * m + j
                    pe.wait_ge(ring_full[p0 % NSLOT], 16 * pair + 16 * (p0 // NSLOT + 1))
                    w = slot(p0, KD)
                    for k in range(KD):
                        last = mm(ps[:, bank, :], hgT[:, k, :], w[:, k, :], k == 0, k == KD - 1)
                    last.then_inc(S[("gate_done", "up_done")[j]], 1)

            def act_transpose(n):
                pe.wait_ge(S["act_ready"], n + 1)
                for k in range(C):
                    last = pe.transpose(ps[:, 3, k * P:(k + 1) * P], AC[:, k * P:(k + 1) * P], ident)
                last.then_inc(S["act_T"], 1)

            def scatter(n, b, last_of_pass=False):
                pe.wait_ge(S["down_sb"], 2 * n + 2)
                for r in range(6):
                    i, half = r // 2, r % 2
                    if r >= 2 or last_of_pass:
                        pe.wait_ge(S["y_added"], 6 * n + (r - 1))
                    mm(ps[:, (7, 2)[r % 2], :], SelWT[:, b, i * P:(i + 1) * P], DN[:, half * 512:(half + 1) * 512]).then_inc(S["scattered"], 1)

            def down(n, m, pair):
                p0 = FIRST_EXPERT + 3 * m + 2
                pe.wait_ge(S["act_T_sb"], n + 1)
                pe.wait_ge(ring_full[p0 % NSLOT], 16 * pair + 16 * (p0 // NSLOT + 1))
                w = slot(p0, C)
                for half in range(2):
                    for k in range(C):
                        last = mm(ps[:, 5 + half, :], ACT_T[:, k, :], w[:, k, half * 512:(half + 1) * 512], k == 0, k == C - 1)
                last.then_inc(S["down_done"], 1)

            def expert_pass(base):
                pair0 = base // 2
                gather(base, base > 0)
                if base:
                    pe.wait_ge(S["y_added"], 6 * base)
                gate_up(base, 0, pair0)
                act_transpose(base)
                gather(base + 1, base > 0)
                down(base, 0, pair0)
                with pe.Fori(0, NPAIR - 1) as i:
                    for m in (1, 2):
                        n = 2 * i + (base + m)
                        pair = i + (pair0 + m // 2)
                        gate_up(n, m % 2, pair)
                        scatter(n - 1, 1 - m % 2)
                        act_transpose(n)
                        gather(n + 1)
                        down(n, m % 2, pair)
                n = base + NE - 1
                gate_up(n, 1, pair0 + NPAIR - 1)
                scatter(n - 1, 0)
                act_transpose(n)
                down(n, 1, pair0 + NPAIR - 1)
                scatter(n, 1, True)

            pe.wait_ge(S["route_ready"], 1)
            expert_pass(0)
            over = pe.value_load(over_i[0:1, 0:1], min_val=0, max_val=T)
            with pe.If(over > P):
                expert_pass(NE)
                expert_pass(2 * NE)

        @block.vector
        def _(dve):
            done = {}

            def step(ins, name="dve"):
                done[name] = done.get(name, 0) + 1
                ins.then_inc(S[name], 1)
                dve.wait_ge(S[name], done[name])

            tt, ts, stt = dve.tensor_tensor, dve.tensor_scalar, dve.scalar_tensor_tensor
            step(dve.memset(ones, 1.0))
            step(dve.memset(mean_w, 1.0 / P))
            step(dve.memset(eps, EPS))
            step(dve.memset(zeros4, 0.0))
            dve.wait_ge(S["x_in"], 32)
            dve.wait_ge(S["pos_in"], 16)
            step(tt(x_in[:, 1:3, :], x_in[:, 1:3, :], pos_in, ALU.add), "pos_added")

            dve.wait_ge(S["z_taken"], 1)
            raw = colsB[:, B_LB:B_LB + 8]
            t = [tiny_tmp[:, 8 * n:8 * n + 8] for n in range(3)]
            lam = colsB[:, B_LAM:B_LAM + 8]
            step(tt(t[0], raw, raw, ALU.subtract), "lb_diff")
            step(stt(nsp, lam, -1.0, lam, ALU.mult, ALU.max), "lam_abs")
            dve.wait_ge(S["lb_exp"], 1)
            step(dve.reciprocal(t[1], t[0]))
            step(tt(t[0], t[0], t[1], ALU.mult))
            step(tt(lb, t[0], t[0], ALU.subtract))
            step(ts(om_lb, lb, -1.0, 1.0, ALU.mult, ALU.add))
            step(ts(neg_om_lb, om_lb, -1.0, None, ALU.mult))
            for c in range(C):
                k = A_BIN + 4 * WIN_COL["mk"] + c
                step(ts(tiny_tmp[:, 28 + c:29 + c], colsA[:, k:k + 1], KSCALE, None, ALU.mult))

            dve.wait_ge(S["z_taken"], Z_INDEX[("ada_col", 3)] + 1)
            step(tt(modc[:, 0:16, :], modc[:, 0:16, :], colsA[:, A_ADA:A_ADA + 16].unsqueeze(2).broadcast_to([P, 16, 2]), ALU.add))
            step(ts(sc1p, modc[:, 8:16, :], 1.0, None, ALU.add))
            for k in range(KD):
                for s, (t0, t1) in enumerate(SPANS):
                    step(ts(hT[:, k, t0:t1], hT[:, k, t0:t1], sc1p[:, k, s:s + 1], modc[:, k, s:s + 1], ALU.mult, ALU.add), "h_ready")

            dve.wait_ge(S["lam_exp"], 1)
            e = t[0]
            step(ts(t[1], nsp, 2.0, None, ALU.add))
            step(dve.reciprocal(t[1], t[1]))
            step(tt(e, nsp, t[1], ALU.mult))
            step(tt(t[1], e, e, ALU.mult))
            step(ts(t[2], t[1], 1.0 / 17, None, ALU.mult))
            for odd in (15, 13, 11, 9, 7, 5, 3):
                step(stt(t[2], t[2], 1.0 / odd, t[1], ALU.add, ALU.mult))
            step(stt(t[2], t[2], 1.0, e, ALU.add, ALU.mult))
            step(ts(t[1], lam, -1.0, 0.0, ALU.mult, ALU.max))
            step(stt(t[2], t[2], 2.0, t[1], ALU.mult, ALU.add))
            step(ts(nsp, t[2], -8.0, None, ALU.mult))
            step(ts(psp, t[2], 8.0, None, ALU.mult), "sp_ready")

            dve.wait_ge(S["z_taken"], Z_INDEX[("chan", "rx", C - 1)] + 1)
            for c in range(C):
                x, o = chunk(RX, c), chunk(XC, c)
                w = [colsA[:, A_CONVW + 4 * n + c:A_CONVW + 4 * n + c + 1] for n in range(4)]
                step(ts(o, x, w[2], colsA[:, A_CONVB + c:A_CONVB + c + 1], ALU.mult, ALU.add))
                for n, sh in ((0, -2), (1, -1), (3, 1)):
                    for s0, s1 in SPANS:
                        lo, hi = max(s0, s0 - sh), min(s1, s1 - sh)
                        step(stt(o[:, lo:hi], x[:, lo + sh:hi + sh], w[n], o[:, lo:hi], ALU.mult, ALU.add),
                             "rx_conv" if (c, n, s0) == (C - 1, 3, SEQ) else "dve")

            dve.wait_ge(S["z_taken"], Z_INDEX[("chan", "rg", C - 1)] + 1)
            for c in range(C):
                dve.wait_ge(S["lru_act"], 4 * c + 4)
                step(ts(LT, R_, 1.0, None, ALU.add))
                step(dve.reciprocal(LT, LT))
                step(stt(R_, R_, 0.0, LT, ALU.max, ALU.mult), "lru_den")
                for d in range(2):
                    step(tt(I_[:, d * T:(d + 1) * T], I_[:, d * T:(d + 1) * T], chunk(XC, c), ALU.mult))
                dve.wait_ge(S["lru_sqrt"], c + 1)
                step(tt(I_, I_, R_, ALU.mult))
                for d in range(2):
                    for s, (t0, t1) in enumerate(SPANS):
                        av, uv, hv = [z[:, d * T + t0:d * T + t1] for z in (A_, I_, HB)]
                        if d:
                            av, uv, hv = av[:, ::-1], uv[:, ::-1], hv[:, ::-1]
                        init = colsB[:, B_H0 + 4 * d + c:B_H0 + 4 * d + c + 1] if s else 0.0
                        step(dve.tensor_tensor_scan(hv, av, uv, init, ALU.mult, ALU.add))
                step(dve.tensor_copy(h_fin[:, 0, c:c + 1], HB[:, SEQ - 1:SEQ]))
                step(dve.tensor_copy(h_fin[:, 1, c:c + 1], HB[:, T:T + 1]))
                step(tt(LT[:, 0:T], HB[:, 0:T], HB[:, T:2 * T], ALU.add))
                step(tt(chunk(YR, c), chunk(YR, c), LT[:, 0:T], ALU.mult), "lru_done")

            dve.wait_ge(S["z_taken"], Z_INDEX[("chan", "gfb", C - 1)] + 1)
            for d, (f, kb) in enumerate(((FF, KBF), (FB, KBB))):
                for h in range(H):
                    k = 4 * d + h
                    step(ts(chunk(kb, h), chunk(f, h), neg_om_lb[:, k:k + 1], om_lb[:, k:k + 1], ALU.mult, ALU.add))
                    step(ts(chunk(f, h), chunk(f, h), om_lb[:, k:k + 1], lb[:, k:k + 1], ALU.mult, ALU.add))
                step(ts(f, f, TINY, None, ALU.max), "dve" if d == 0 else "hg_start")
            step(tt(QFB, QFF, FB, ALU.mult))
            dve.wait_ge(S["masks_cast"], 1)
            dve.wait_ge(S["consts_in"], 16)
            taken = [0]

            def scores_in():
                taken[0] += 1
                dve.wait_ge(S["hg_scores"], taken[0])
                return ps[:, 4 + (taken[0] - 1) % 4, :].rearrange("p (h t) -> p h t", h=H)

            for i in range(NT):
                step(tt(SCO[:, i], scores_in(), ident.unsqueeze(1).broadcast_to([P, H, P]), ALU.mult), "hg_taken")
            step(tt(QFF, QFF, FF, ALU.mult), "hg_level")

            for lv in range(LEVELS):
                h = 1 << lv
                for i in range(NT):
                    for d in range(2):
                        m = hg_masks[:, d, lv, :].unsqueeze(1).broadcast_to([P, H, P])
                        step(dve.copy_predicated(SCO[:, i], m, scores_in()), "hg_taken")
                for q, kb, f, right_q in ((QFF, KBF, FF, 1), (QFB, KBB, FB, 0)):
                    qh, kh = halves(q, h), halves(kb, h)
                    fl = f[:, 0::2 * h].unsqueeze(2)
                    fr = f[:, h::2 * h].unsqueeze(2)
                    shape = [P, U // (2 * h), h]
                    first, last = (fl, fr) if right_q else (fr, fl)
                    step(tt(qh[right_q], qh[right_q], first.broadcast_to(shape), ALU.mult))
                    step(tt(kh[1 - right_q], kh[1 - right_q], last.broadcast_to(shape), ALU.mult))
                    step(tt(f[:, 0::2 * h], f[:, 0::2 * h], f[:, h::2 * h], ALU.mult), "dve" if right_q else "hg_level")
            for d in range(2):
                step(dve.tensor_copy(SCX[:, d], scores_in()), "hg_taken")
            for name, q, f, far, near in (("dve", QFF, FF, 2, 1), ("hg_final", QFB, FB, 1, 2)):
                qv = q.rearrange("p (h t) -> p h t", h=H)
                fv = f.rearrange("p (h t) -> p h t", h=H)
                step(tt(qv[:, :, far * P:(far + 1) * P], qv[:, :, far * P:(far + 1) * P],
                        fv[:, :, near * P:near * P + 1].broadcast_to([P, H, P]), ALU.mult), name)

            dve.wait_ge(S["z_taken"], len(Z_INDEX))
            step(tt(modc[:, 16:48, :], modc[:, 16:48, :], colsA[:, A_ADA + 16:A_ADA + 48].unsqueeze(2).broadcast_to([P, 32, 2]), ALU.add), "mod2_ready")
            dve.wait_ge(S["gate_w_in"], 32)
            step(tt(gz, gz, gbias.unsqueeze(1).broadcast_to([P, NT, 16]), ALU.add), "gz_ready")

            for h in range(H):
                dve.wait_ge(S["o_std"], h + 1)
                b = h % 2
                step(dve.reciprocal(O_STD[:, b, :], O_STD[:, b, :]))
                step(tt(O_STD[:, b, :], ps[:, 4 + b, 0:T], O_STD[:, b, :], ALU.mult))
                step(stt(chunk(YH, h), O_STD[:, b, :], colsA[:, A_HGG + h:A_HGG + h + 1], chunk(YH, h), ALU.mult, ALU.mult), "o_norm")

            dve.wait_ge(S["gz_rows"], 4)
            step(stt(FE, GF, -1.0, GF, ALU.mult, ALU.max), "f_abs")
            step(ts(GF, GF, 0.0, None, ALU.min))
            dve.wait_ge(S["f_ln"], 1)
            step(tt(GF, GF, FE, ALU.subtract))
            for d in range(2):
                for t0, t1 in SPANS:
                    src, dst = GF[:, d, t0:t1], BR[:, d, t0:t1]
                    if d:
                        src, dst = src[:, ::-1], dst[:, ::-1]
                    step(dve.tensor_tensor_scan(dst, src, zeros4[0:H, 0:t1 - t0], 0.0, ALU.add, ALU.add))
            step(tt(CR, GI, BR, ALU.subtract))
            dve.wait_ge(S["mini_in"], 48)
            for d in range(2):
                for s, (t0, t1) in enumerate(SPANS):
                    src, dst = CR[:, d, t0:t1], MR[:, d, t0:t1]
                    if d:
                        src, dst = src[:, ::-1], dst[:, ::-1]
                    step(dve.tensor_tensor_scan(dst, src, src, m0_rows[0:H, d:d + 1] if s else 0.0, ALU.max, ALU.max))
            step(stt(NBM, BR, -1.0, MR, ALU.mult, ALU.subtract))
            step(ts(m_fin[0:H, 0:1], NBM[:, 0, SEQ - 1:SEQ], -1.0, None, ALU.mult))
            step(ts(m_fin[0:H, 1:2], NBM[:, 1, 0:1], -1.0, None, ALU.mult), "m_rows")

            dve.wait_ge(S["c_cols"], 1)
            for n in range(8):
                h, d = n // 2, n % 2
                b = n % 2
                dve.wait_ge(S["bc_ready"], n + 1)
                dve.wait_ge(S["si_ready"], n + 1)
                m = ps[:, 0, :]
                pw_ = PW_[:, b, :]
                parts = [(0, 0, P, 0)] + ([(P, P, T, 1), (3 * P, 2 * P, T, 2)] if d == 0 else [(P, P, 2 * P, 1), (2 * P, P, T, 2)])
                for k, (o, t0, t1, i) in enumerate(parts):
                    step(ts(pw_[:, o:o + t1 - t0], m[:, t0:t1], c_cols[:, d, i, h:h + 1], 0.0, ALU.subtract, ALU.max),
                         "p_arg" if k == 2 else "dve")
                step(tt(QS[:, b, :], chunk(MQ, h)[:, SEQ:T], SI[:, b, :], ALU.mult), "qs_ready")
                dve.wait_ge(S["p_exp"], n + 1)
                dve.wait_ge(S["kT_ready"], n + 1)
                last = 0 if d else P - 1
                step(ts(KE[:, b, :], ps[:, 3, 256:384], pw_[:, last:last + 1], None, ALU.mult), "ke_ready")
                dve.wait_ge(S["p_mask"], 2 * n + 2)
                step(tt(WW[:, b, :], pw_, ps[:, 2, :], ALU.mult), "w_ready")
                dve.wait_ge(S["num_ready"], n + 1)
                dve.wait_ge(S["den_abs"], n + 1)
                step(tt(DEN[:, b, :], DEN[:, b, :], FLOOR[:, b, :], ALU.max))
                step(dve.reciprocal(DEN[:, b, :], DEN[:, b, :]))
                if d == 0:
                    step(tt(HS[:, 0, :], ps[:, 4, 0:T], DEN[:, b, :], ALU.mult), "h_done")
                else:
                    step(tt(DEN[:, b, :], ps[:, 4, 0:T], DEN[:, b, :], ALU.mult))
                    step(tt(HS[:, 1, :], HS[:, 0, :], DEN[:, b, :], ALU.add), "h_done")
                    dve.wait_ge(S["hm_ready"], h + 1)
                    step(tt(HS[:, 0, :], HS[:, 1, :], ps[:, 6, 0:T], ALU.subtract), "hc_ready")
                    dve.wait_ge(S["hstd_ready"], h + 1)
                    step(dve.reciprocal(HT2[:, 1, :], HT2[:, 1, :]))
                    step(tt(HT2[:, 1, :], HT2[:, 1, :], HS[:, 0, :], ALU.mult))
                    step(stt(chunk(YM, h), HT2[:, 1, :], colsA[:, A_MLG + h:A_MLG + h + 1], chunk(YM, h), ALU.mult, ALU.mult),
                         "ml_done" if h == H - 1 else "dve")

            def norm(i, v, name):
                x = X1[:, i, :]
                for half in range(2):
                    step(dve.bn_stats(mv_stats[:, 6 * half:6 * half + 6], x[:, half * 512:(half + 1) * 512]))
                step(dve.bn_aggr(mv_stats[:, 12:14], mv_stats[:, 0:12]), name + "_var")
                dve.wait_ge(S[name + "_std"], i + 1)
                step(dve.reciprocal(rstd, rstd))
                step(ts(x, x, mv_stats[:, 12:13], rstd, ALU.subtract, ALU.mult))
                step(tt(x, x, ln_b[:, v, :], ALU.mult))

            dve.wait_ge(S["x2_in"], 32)
            dve.wait_ge(S["pos2_in"], 16)
            step(tt(X1[:, 1:3, :], X1[:, 1:3, :], pos2, ALU.add))
            dve.wait_ge(S["ln_in"], 16 * 8)
            dve.wait_ge(S["bcast_taken"], 16)
            for i in range(NT):
                s = min(i, 1)
                dve.wait_ge(S["y_ready"], 2 * i + 2)
                for half in range(2):
                    cols = slice(half * 512, (half + 1) * 512)
                    step(tt(H2[:, i, cols], ps[:, 2 * i + half, :], g1_b[:, s, cols], ALU.mult))
                step(stt(X1[:, i, :], X1[:, i, :], ALPHA, H2[:, i, :], ALU.mult, ALU.add))
                norm(i, 0, "ln")
                step(tt(X1[:, i, :], X1[:, i, :], ln_b[:, 1, :], ALU.add))
                step(tt(H2[:, i, :], X1[:, i, :], sc2_b[:, s, :], ALU.mult))
                step(tt(H2[:, i, :], H2[:, i, :], sh2_b[:, s, :], ALU.add), "h2_ready")

            def over3(x, n=NE):
                return x.unsqueeze(2).broadcast_to([P, NT, n])

            dve.wait_ge(S["logits_ready"], 1)
            logits = ps[:, 0, 0:48].rearrange("p (i e) -> p i e", i=NT)
            step(dve.tensor_reduce(r3[0], logits, AX.X, ALU.max))
            step(tt(scores, logits, over3(r3[0]), ALU.subtract), "smax_ready")
            dve.wait_ge(S["sexp_ready"], 1)
            step(dve.tensor_reduce(r3[1], scores, AX.X, ALU.add))
            step(dve.reciprocal(r3[2], r3[1]))
            step(tt(scores, scores, over3(r3[2]), ALU.mult))
            step(tt(sel, scores, b_router.unsqueeze(1).broadcast_to([P, NT, NE]), ALU.add))
            sv = sel.rearrange("p i (g e) -> p i g e", g=NG)
            e0, e1, e2, e3 = [sv[:, :, :, n] for n in range(4)]
            step(tt(g12[0], e0, e1, ALU.max))
            step(tt(g12[1], e0, e1, ALU.min))
            step(tt(g12[2], e2, e3, ALU.max))
            step(tt(g12[3], e2, e3, ALU.min))
            step(tt(g12[4], g12[0], g12[2], ALU.max))
            step(tt(g12[5], g12[0], g12[2], ALU.min))
            step(tt(g12[6], g12[1], g12[3], ALU.max))
            step(tt(g12[5], g12[5], g12[6], ALU.max))
            step(tt(g12[4], g12[4], g12[5], ALU.add))

            def first_max(out, x, tmp, n):
                step(dve.tensor_reduce(r3[3], x, AX.X, ALU.max))
                step(tt(tmp, x, over3(r3[3], n), ALU.is_equal))
                step(tt(tmp, tmp, desc16[:, 0:n].unsqueeze(1).broadcast_to([P, NT, n]), ALU.mult))
                step(dve.tensor_reduce(r3[4], tmp, AX.X, ALU.max))
                step(tt(out, tmp, over3(r3[4], n), ALU.is_equal))

            first_max(g12[0], g12[4], g12[1], NG)
            step(ts(g12[1], g12[0], BIG, -BIG, ALU.mult, ALU.add))

            def per_expert(x):
                return x.unsqueeze(3).broadcast_to([P, NT, NG, NG])

            def grouped(x):
                return x.rearrange("p i (g e) -> p i g e", g=NG)

            step(tt(grouped(masked), sv, per_expert(g12[0]), ALU.mult))
            step(tt(grouped(masked), grouped(masked), per_expert(g12[1]), ALU.add))
            first_max(oh1, masked, t16a, NE)
            step(stt(masked, oh1, -3e38, masked, ALU.mult, ALU.add))
            first_max(oh2, masked, t16a, NE)
            step(tt(mask, oh1, oh2, ALU.add), "mask_ready")
            step(tt(comb, scores, mask, ALU.mult))
            step(dve.tensor_reduce(r3[1], comb, AX.X, ALU.add))
            step(dve.reciprocal(r3[2], r3[1]))
            step(tt(PW[:, :, :, 1].rearrange("p e i -> p i e"), comb, over3(r3[2]), ALU.mult))
            dve.wait_ge(S["ranks_ready"], 1)
            step(tt(ranks, ps[:, 1, 0:48].rearrange("p (i e) -> p i e", i=NT), mask, ALU.mult))
            step(ts(t16a, mask, 4096.0, -4096.0, ALU.mult, ALU.add))
            step(tt(PW[:, :, :, 0].rearrange("p e i -> p i e"), ranks, t16a, ALU.add))
            step(dve.tensor_reduce(over_f[:, 0:1], ps[:, 1, 48:64], AX.X, ALU.max))
            step(dve.tensor_copy(over_i[:, 0:1], over_f[:, 0:1]))
            step(dve.memset(YACC, 0.0), "route_ready")

            def select(n, e):
                dve.tensor_copy(pw, PW[:, bass.ds(e, 1)].rearrange("p a i w -> p (a i) w")).then_inc(S["sel_cols"], 1)
                dve.wait_ge(S["sel_cols"], n + 1)
                for i in range(NT):
                    ts(Sel[:, i, :], iota, pw[:, i, 0:1], None, ALU.is_equal)
                    ins = ts(SelW[:, i, :], iota, pw[:, i, 0:1], pw[:, i, 1:2], ALU.is_equal, ALU.mult)
                ins.then_inc(S["sel_ready"], 1)

            def gated(n):
                dve.wait_ge(S["sg_ready"], n + 1)
                tt(AC, SG, ps[:, 4, :], ALU.mult).then_inc(S["act_ready"], 1)

            def add_back(n):
                for r in range(6):
                    i, half = r // 2, r % 2
                    dve.wait_ge(S["scattered"], 6 * n + (r + 1))
                    yv = YACC[:, i, half * 512:(half + 1) * 512]
                    tt(yv, yv, ps[:, (7, 2)[r % 2], :], ALU.add).then_inc(S["y_added"], 1)

            def expert_pass(base):
                select(base, 0)
                dve.wait_ge(S["gathered"], base + 1)
                select(base + 1, 1)
                gated(base)
                with dve.Fori(0, NPAIR - 1) as i:
                    for m in (1, 2):
                        n = 2 * i + (base + m)
                        dve.wait_ge(S["gathered"], n + 1)
                        select(n + 1, 2 * i + (m + 1))
                        gated(n)
                        add_back(n - 1)
                n = base + NE - 1
                gated(n)
                add_back(n - 1)
                add_back(n)

            expert_pass(0)
            over = dve.value_load(over_i[0:1, 0:1], min_val=0, max_val=T)
            with dve.If(over > P):
                for base in (NE, 2 * NE):
                    dve.wait_ge(S["gathered"], base)
                    ts(PW[:, :, :, 0], PW[:, :, :, 0], -float(P), None, ALU.add).then_inc(S["over_shift"], 1)
                    dve.wait_ge(S["over_shift"], base // NE)
                    expert_pass(base)

            for i in range(NT):
                s = min(i, 1)
                step(tt(YACC[:, i, :], YACC[:, i, :], g2_b[:, s, :], ALU.mult))
                step(stt(X1[:, i, :], X1[:, i, :], ALPHA, YACC[:, i, :], ALU.mult, ALU.add))
                norm(i, 2, "ln2")
                step(tt(X1[:, i, :], X1[:, i, :], ln_b[:, 3, :], ALU.add), "out_tile")


_INS = ["x_prompt", "x_sample", "state_lru_h", "state_hgrn_S", "state_mlstm_C", "state_mlstm_n", "state_mlstm_m", "c", "c_ctx",
        "w_ada", "b_ada", "w_in", "b_in", "conv_w", "conv_b", "lru_wa", "lru_ba", "lru_wx", "lru_bx", "lru_lam", "hg_lb",
        "hg_norm_g", "ml_norm_g", "w_out", "ln1_g", "ln1_b", "ln2_g", "ln2_b", "w_router", "b_router", "w_gate", "w_up", "w_down"]
_OUTS = [(1, SEQ, D), (1, LAT, D), (1, 1, 2, G), (1, 1, 2, H, P, P), (1, 1, 2, H, P, P), (1, 1, 2, H, P), (1, 1, 2, H)]


def _constants():
    import numpy as np

    r = np.arange(P)
    consts = np.zeros((P, 400), np.float32)
    consts[:, 0:128] = r[:, None] == r[None, :]
    consts[:, 128:256] = r[:, None] < r[None, :]
    consts[:, 256:384] = r[None, :]
    consts[:, 384:400] = 16 - np.arange(16)[None, :]
    masks = np.zeros((P, 2, LEVELS, P), np.float32)
    for lv in range(LEVELS):
        same = (r[:, None] >> (lv + 1)) == (r[None, :] >> (lv + 1))
        left = ((r >> lv) & 1) == 0
        masks[:, 0, lv] = same & left[:, None] & ~left[None, :]
        masks[:, 1, lv] = same & ~left[:, None] & left[None, :]
    q = D // 4
    freq = np.exp(np.float32(-np.log(10000.0)) * np.arange(q, dtype=np.float32) / np.float32(q)).astype(np.float32)
    tok = np.arange(LAT)
    ar = (tok // 64).astype(np.float32)[:, None] * freq
    ac = (tok % 64).astype(np.float32)[:, None] * freq
    pos = np.concatenate([np.sin(ar), np.cos(ar), np.sin(ac), np.cos(ac)], axis=-1).astype(np.float32)
    return {"consts": consts, "hg_masks": masks.reshape(P, -1), "pos": pos}


def kernel(**inputs):
    import numpy as _np
    import concourse.bacc as _bacc
    from concourse import mybir as _mybir
    from concourse.bass_utils import run_bass_kernel_spmd as _run

    nc = _bacc.Bacc("TRN2", target_bir_lowering=False, num_devices=1)
    arrays, args = {}, {}
    named = {name: _np.ascontiguousarray(inputs[name]) for name in _INS}
    named.update(_constants())
    for name, value in named.items():
        arrays[f"in_{name}"] = value
        args[name] = nc.dram_tensor(f"in_{name}", value.shape, _mybir.dt.from_np(value.dtype), kind="ExternalInput").ap()
    outs = [nc.dram_tensor(f"out_{i}", shape, _mybir.dt.float32, kind="ExternalOutput").ap() for i, shape in enumerate(_OUTS)]
    build(nc, args, outs)
    r = _run(nc, [arrays], core_ids=[0])
    return tuple(r.results[0][f"out_{i}"] for i in range(len(_OUTS)))
```

```python
from contextlib import ExitStack

import concourse.bass as bass
from concourse import mybir

F32 = mybir.dt.float32
F32R = mybir.dt.float32r
I32 = mybir.dt.int32
U8 = mybir.dt.uint8
ALU = mybir.AluOpType
ACT = mybir.ActivationFunctionType
AX = mybir.AxisListType

P = 128
D = 1024
KD = D // P
G = 512
C = G // P
SEQ = 128
LAT = 256
T = SEQ + LAT
NT = T // P
SPANS = [(0, SEQ), (SEQ, T)]
H = 4
NE = 16
NG = 4
NPAIR = NE // 2
D_IN = 11 * G + 16
GATE_OFF = 11 * G
ALPHA = 2.0 ** 0.25
EPS = 1e-5
TINY = 1e-30
BIG = 1e30
KSCALE = float(P) ** -0.5
U = C * T
LEVELS = 7
PIECE = 4096
NSLOT = 3
UNIT = PIECE // 4
POOL_Q = ((3,), (1, 3), (1, 3))

ADA = [n if n < 4 else 11 + n for n in range(12)]
WIN_ORDER = ["rx", "rg", "gq", "gff", "gfb", "gi", "go", "mq", "mk", "mv", "mo"]
WIN_COL = {"rx": 0, "rg": 1, "gq": 2, "gff": 3, "gfb": 4, "gi": 5, "go": 6, "mq": 7, "mk": 8, "mv": 9, "mo": 10}
WIN = {g: 4 + n for n, g in enumerate(WIN_ORDER)}
WOUT = [23, 24, 25]
FIRST_EXPERT = 26

A_BIN, A_ADA, A_CONVW, A_CONVB, A_HGG, A_MLG, A_ROWS = 0, 44, 92, 108, 112, 116, 120
B_BA, B_BX, B_LAM, B_LB, B_H0, B_N0, B_C, B_ROWS = 0, 8, 16, 24, 32, 40, 48, 64
SH1, SC1, G1, SH2, SC2, G2 = range(6)

SEMS = (
    "rows_in x_in pos_in consts_in masks_in masks_cast gate_w_in lru_w_in vbias_in mini_in s0_in c0_in x2_in pos2_in ln_in out_h "
    "out_S out_C out_n out_m out_y z_ready lb_diff lb_exp lam_abs lam_exp z_taken silu_c silu_c2 pos_added cols_ready mod1_ready h_ready "
    "rx_conv sp_ready lru_w_ready lru_zeroed gates_ready gates_taken lru_act lru_den lru_sqrt lru_done vbias_added "
    "dve pool hg_start hg_qk hg_scores hg_taken hg_level hg_final kb_T kb_T_sb s_fin s_fin_sb o_ready o_sq o_var o_std "
    "o_norm gz_ready gz_rows gz_rows_T f_abs f_exp f_ln m_rows c_T c_cols bc_ready p_arg p_exp p_mask kT_ready ke_ready "
    "kT_sb cfin_ready cfin_sb w_ready si_ready qs_ready num_ready ml_scores den_floor den_abs h_done hm_ready hc_ready hsq_ready hv_ready "
    "hstd_ready ml_done mod2_ready bcast_ready bcast_taken g2_moved y_ready ln_var ln_std h2_ready h2_T h2_T_sb logits_ready "
    "smax_ready sexp_ready mask_ready ranks_ready route_ready sel_cols sel_ready g_rows g_rows_sb g_rows_T gathered gather_taken "
    "sg_ready act_ready act_T act_T_sb down_done down_sb hi_ready lo_pool lo_dve unit_used h_hi h_lo hg_lo act_lo down_lo h2_hi h2_lo scattered y_added ln2_var ln2_std out_tile over_shift"
).split()


LATE_ADA = [(), (), (4, 5), (6,), (7, 8), (9,), (10,), (11,)]


def z_jobs():
    turns = [("xT", i, half) for i in range(NT) for half in range(2)]

    def ada(first, last):
        out = []
        for n in range(first, last + 1):
            if n < last:
                out.append(("ada_row", n))
            if n > first:
                out.append(("ada_col", n - 1))
        return out

    def group(g):
        if g in ("gi", "mv"):
            return [("tok", g)]
        return [("chan", g, c) for c in range(C)]

    early = ada(0, 4)
    jobs = [("rows",)] + turns[:3] + early[:1] + turns[3:] + early[1:] + [("gates",)]
    for g in ("rx", "rg", "gq"):
        jobs += group(g)
    jobs += [("lru", 0)] + group("gff")[:1] + [("lru2", 0)] + group("gff")[1:]
    jobs += [("lru", 1)] + group("gfb")[:1] + [("lru2", 1)] + group("gfb")[1:]
    jobs += [("lru", 2)] + group("gi") + [("lru2", 2)]
    jobs += [("lru", 3)] + group("go")[:1] + [("lru2", 3)] + group("go")[1:]
    jobs += group("mq") + group("mk") + [("hg_diag",)]
    late = ada(4, 12)
    for n in range(LEVELS + 1):
        if n < 2:
            jobs += group(("mv", "mo")[n])
        jobs += [job for job in late if job[0] == "ada_row" and job[1] in LATE_ADA[n] or job[0] == "ada_col" and job[1] + 1 in LATE_ADA[n]]
        if n == LEVELS:
            jobs.append(late[-1])
        jobs.append(("hg_level", n))
    return jobs


JOBS = z_jobs()
Z_KINDS = ("rows", "xT", "ada_row", "ada_col", "tok", "chan", "gates")
Z_INDEX = {}
Z_COUNT = 0
for _job in JOBS:
    if _job[0] in Z_KINDS:
        Z_INDEX[_job] = Z_COUNT
        Z_COUNT += NT if _job[0] == "tok" else 1


def job_units(job):
    if job[0] == "ada_row":
        return list(range(4 * ADA[job[1]], 4 * ADA[job[1]] + 4))
    if job[0] == "tok":
        return list(range(4 * WIN[job[1]], 4 * WIN[job[1]] + 4))
    if job[0] == "chan":
        return [4 * WIN[job[1]] + job[2]]
    return []


USED = {}
BY_COLUMN = {}
MIX_USED = 0
for _job in JOBS:
    _units = job_units(_job)
    for _u in _units:
        BY_COLUMN[_u] = _job[0] == "chan"
        if _u != _units[-1]:
            MIX_USED += 1
            USED[_u] = ("unit_used", MIX_USED)
        else:
            USED[_u] = ("z_ready", Z_INDEX[_job] + (NT if _job[0] == "tok" else 1))
MIX_UNITS = len(USED)
DVE_MIX = [u for n in ADA for u in range(4 * n, 4 * n + 4) if u % 2]


def mix_lo(last):
    dve_n = sum(u <= last for u in DVE_MIX)
    return last + 1 - dve_n, dve_n


MIX_POOL, MIX_DVE = mix_lo(MIX_UNITS - 1)

POOL_N = sum(len(q) for q in POOL_Q)
DVE_N = 12 - POOL_N


def lo_counts(j, q):
    pool_n = sum(len(x) for x in POOL_Q[:j]) + sum(x < q for x in POOL_Q[j])
    return pool_n, 4 * j + q - pool_n


def halves(ap, h):
    v = ap.rearrange("p (b x) -> p b x", x=2 * h)
    return v[:, :, 0:h], v[:, :, h:2 * h]


def build(nc, a, outs):
    with ExitStack() as ctx:
        def sb(name, shape, dt=F32):
            return ctx.enter_context(nc.sbuf_tensor(name, shape, dt))

        S = {n: ctx.enter_context(nc.semaphore(n)) for n in SEMS}
        ring_full = [ctx.enter_context(nc.semaphore(f"ring_full{n}")) for n in range(NSLOT)]

        base = (nc.sbuf_base + 31) // 32 * 32
        words = 53200
        ctx.enter_context(nc.sbuf_tensor("fence", [P, words], F32))

        def place(name, off, n, dt=F32):
            assert off + n <= words
            return nc.alloc_sbuf_tensor_at(name, [P, n], dt, offset=base + 4 * off)[:, :]

        arena = place("arena", 0, 16 * U)
        small = place("small", 16 * U, 912)
        h_hi = place("h_hi", 16 * U + 912, KD * T, F32R)
        h_lo = place("h_lo", 16 * U + 912 + KD * T, KD * T, F32R)
        o_conv = 16 * U + 912 + 2 * KD * T
        w_hi = place("w_hi", o_conv, PIECE, F32R).rearrange("p (q n) -> p q n", q=4)
        w_lo = place("w_lo", o_conv + PIECE, PIECE, F32R).rearrange("p (q n) -> p q n", q=4)
        ring = place("ring", o_conv + 2 * PIECE, NSLOT * PIECE).rearrange("p (s n) -> p s n", s=NSLOT)
        silu_hi = place("silu_hi", o_conv + (2 + NSLOT) * PIECE + 1024, 16, F32R)
        silu_lo = place("silu_lo", o_conv + (2 + NSLOT) * PIECE + 1040, 16, F32R)
        extra = place("extra", o_conv + (2 + NSLOT) * PIECE, 1024)
        ps = ctx.enter_context(nc.psum_tensor("ps", [P, 8, 512], F32))

        at = [0]

        def carve(n):
            at[0] += n
            assert at[0] <= 912
            return small[:, at[0] - n:at[0]]

        def unit(i, off=0, n=U):
            return arena[:, i * U + off:i * U + off + n]

        ident = carve(128)
        ones = carve(128)
        colsA = carve(A_ROWS)
        colsB = carve(B_ROWS)
        modc = carve(96).rearrange("p (v s) -> p v s", s=2)
        sc1p = carve(16).rearrange("p (v s) -> p v s", s=2)
        silu_cols = carve(16)
        h_fin = carve(8).rearrange("p (d c) -> p d c", d=2)
        lb = carve(8)
        om_lb = carve(8)
        neg_om_lb = carve(8)
        psp = carve(8)
        nsp = carve(8)
        tiny_tmp = carve(32)
        eps = carve(1)
        c_cols = carve(24).rearrange("p (d i h) -> p d i h", d=2, i=NT)
        m0_rows = carve(2)
        m0_cols = carve(8)
        m_fin = carve(2)
        n_fin = carve(8)
        gz = carve(48).rearrange("p (i g) -> p i g", i=NT)
        gbias = carve(16)
        mv_stats = carve(14)
        w_router = carve(128).rearrange("p (k e) -> p k e", k=KD)
        rstd = carve(1)

        x_in = arena[:, 8 * U:8 * U + NT * D].rearrange("p (i d) -> p i d", i=NT)
        pos_in = arena[:, 10 * U:10 * U + 2 * D].rearrange("p (i d) -> p i d", i=2)
        ada_rows = extra.rearrange("p (b n) -> p b n", b=2)
        hT = arena[:, 4 * U:6 * U].rearrange("p (k t) -> p k t", k=KD)
        HH, HL = [x.rearrange("p (k t) -> p k t", k=KD) for x in (h_hi, h_lo)]
        rowsA = unit(0, 0, 128)
        rowsB = unit(0, 128, 128)
        w_bd = arena[:, 11 * U + 512:11 * U + 512 + 16 * P].rearrange("p (d g c e) -> p d g c e", d=2, g=2, c=C)
        RX, XC = unit(0), unit(1)
        R_, I_ = unit(2, 0, 768), unit(2, 768, 768)
        A_ = unit(3, 0, 768)
        LT, HB = unit(0, 0, 768), unit(0, 768, 768)
        zeros4 = unit(3, 1024, 256)
        gate_w = unit(3, 1280, 128).rearrange("p (k g) -> p k g", k=KD)
        mean_w = unit(3, 1408, 128)
        QFF, FF, FB = unit(4), unit(5), unit(6)
        QFB, KBF, KBB = unit(0), unit(1), unit(2)
        VH = unit(7).rearrange("p (i n) -> p i n", i=NT)
        S0 = unit(3, 0, 1024).rearrange("p (x e) -> p x e", x=8)
        SCO = unit(11).rearrange("p (i h t) -> p i h t", i=NT, h=H)
        SCX = unit(12, 0, 1024).rearrange("p (d h t) -> p d h t", d=2, h=H)
        hg_masks = unit(12, 1024, 448).bitcast(U8).rearrange("p (d l t) -> p d l t", d=2, l=LEVELS)
        masks_wide = arena[:, 14 * U:14 * U + 2 * LEVELS * P]
        YR, YH, YM = unit(13), unit(14), unit(15)
        MQ, MK = unit(8), unit(9)
        MV = unit(10).rearrange("p (i n) -> p i n", i=NT)
        S_FIN = unit(6, 0, 1024).rearrange("p (x e) -> p x e", x=8)
        KB_T = unit(5, 1024, 512).rearrange("p (b s) -> p b s", b=4)
        O_SQ = unit(2, 0, 768).rearrange("p (b t) -> p b t", b=2)
        O_STD = unit(1, 0, 768).rearrange("p (b t) -> p b t", b=2)
        gate_rows = place("gate_rows", 16 * U + 912, 7 * 768)
        GI, GF, BR, CR, MR, NBM, FE = [gate_rows[0:H, 768 * n:768 * n + 768].rearrange("p (d t) -> p d t", d=2) for n in range(7)]
        KTOK = extra[:, 0:512]
        C0 = unit(5, 0, 1024).rearrange("p (x e) -> p x e", x=8)
        PW_ = unit(11, 0, 1024).rearrange("p (b x) -> p b x", b=2)
        WW = arena[:, 11 * U + 1024:11 * U + 2048].rearrange("p (b x) -> p b x", b=2)
        QS = unit(3, 0, 512).rearrange("p (b x) -> p b x", b=2)
        SI = unit(3, 512, 512).rearrange("p (b x) -> p b x", b=2)
        FLOOR = unit(2, 0, 768).rearrange("p (b x) -> p b x", b=2)
        DEN = unit(2, 768, 768).rearrange("p (b x) -> p b x", b=2)
        HS = unit(4, 0, 768).rearrange("p (b x) -> p b x", b=2)
        HT2 = unit(4, 768, 768).rearrange("p (b x) -> p b x", b=2)
        KE = unit(5, 1024, 256).rearrange("p (b x) -> p b x", b=2)
        C_FIN = unit(7, 0, 1024).rearrange("p (x e) -> p x e", x=8)

        def moe(off, n):
            return arena[:, off:off + n]

        X1 = moe(0, 3072).rearrange("p (i d) -> p i d", i=NT)
        H2 = moe(3072, 3072).rearrange("p (i d) -> p i d", i=NT)
        g1_b, sc2_b, sh2_b, g2_made = [place(name, o_conv + 2048 * n, 2048).rearrange("p (s d) -> p s d", s=2)
                              for n, name in enumerate(("gain1_rows", "scale2_rows", "shift2_rows", "gain2_rows"))]
        g2_b = moe(12288, 2048).rearrange("p (s d) -> p s d", s=2)
        ln_b = moe(14336, 4096).rearrange("p (v d) -> p v d", v=4)
        pos2 = moe(3072 + 1024, 2048).rearrange("p (i d) -> p i d", i=2)
        h2T = extra.rearrange("p (k t) -> p k t", k=KD)
        GT = extra.rearrange("p (x n) -> p x n", x=2)
        H2H, H2L = [x.rearrange("p (i d) -> p i d", i=NT) for x in (h_hi, h_lo)]
        YACC = moe(19968, 3072).rearrange("p (i d) -> p i d", i=NT)

        def tok16(n):
            return moe(18432 + 48 * n, 48).rearrange("p (i e) -> p i e", i=NT)

        scores, sel, masked, oh1, oh2, mask, comb, t16a, t16b, ranks, posm = [tok16(n) for n in range(11)]
        g12 = [moe(18960 + 12 * n, 12).rearrange("p (i g) -> p i g", i=NT) for n in range(8)]
        r3 = [moe(19056 + 3 * n, 3) for n in range(6)]
        PW = moe(19074, 96).rearrange("p (e i w) -> p e i w", e=NE, i=NT)
        b_router = moe(19170, 16)
        over_f = moe(19186, 2)
        over_i = moe(19188, 2).bitcast(I32)
        pw = moe(19190, 6).rearrange("p (i w) -> p i w", i=NT)
        desc16 = moe(19200, 16)
        tri = moe(19216, 128)
        iota = moe(19344, 128)

        def parts(name, off, n, k):
            return [place(f"{name}_{x}", off + j * n, n, F32R).rearrange("p (k j) -> p k j", k=k) for j, x in enumerate(("hi", "lo"))]

        HGH, HGL = parts("gathered_tokens", 6144, 1024, KD)
        DNH, DNL = parts("expert_out", 8192, 1024, 2)
        ACH, ACL = parts("expert_act", 10240, 512, C)
        SG = moe(11264, 512)
        AC = moe(11776, 512)
        Sel = place("Sel", 23040, 384, F32R).rearrange("p (i j) -> p i j", i=NT)
        SelT = place("SelT", 23424, 768, F32R).rearrange("p (b t) -> p b t", b=2)
        slot_w = moe(24192, 1)

        def raw_unit(slot, q, by_column):
            if by_column:
                return ring[:, slot, :].rearrange("p (k n) -> p k n", k=KD)[:, :, q * P:(q + 1) * P]
            return ring[:, slot, q * UNIT:(q + 1) * UNIT]

        def part_unit(part, q, by_column):
            return part[:, q, :].rearrange("p (k n) -> p k n", k=KD) if by_column else part[:, q, :]

        def chunk(ap, c):
            return ap[:, c * T:(c + 1) * T]

        block = ctx.enter_context(nc.Block())

        @block.sync
        def _(sp):
            win_v = a["w_in"][0].rearrange("(k p) n -> p k n", p=P)
            ada_v = a["w_ada"][0].rearrange("(k p) n -> p k n", p=P)

            def rows(dst, at_, src, n):
                sp.dma_start(dst[at_:at_ + n, :], src).then_inc(S["rows_in"], 16)

            flat = "(c p) -> c p"
            rows(rowsA, A_BIN, a["b_in"][0, 0:GATE_OFF].rearrange(flat, p=P), 44)
            rows(rowsA, A_ADA, a["b_ada"][0].rearrange(flat, p=P), 48)
            rows(rowsA, A_CONVW, a["conv_w"][0].rearrange("w (c p) -> (w c) p", p=P), 16)
            rows(rowsA, A_CONVB, a["conv_b"][0].rearrange(flat, p=P), 4)
            rows(rowsA, A_HGG, a["hg_norm_g"][0].rearrange(flat, p=P), 4)
            rows(rowsA, A_MLG, a["ml_norm_g"][0].rearrange(flat, p=P), 4)
            for off, name in ((B_BA, "lru_ba"), (B_BX, "lru_bx"), (B_LAM, "lru_lam"), (B_LB, "hg_lb"), (B_H0, "state_lru_h")):
                src = a[name][0, 0] if name == "state_lru_h" else a[name][0]
                rows(rowsB, off, src.rearrange("d (c p) -> (d c) p", p=P), 8)
            rows(rowsB, B_N0, a["state_mlstm_n"][0, 0].rearrange("d h p -> (d h) p"), 8)
            rows(rowsB, B_C, a["c_ctx"].rearrange(flat, p=P), 8)
            rows(rowsB, B_C + 8, a["c"][0].rearrange(flat, p=P), 8)

            def piece(n, src, k):
                if NSLOT <= n < FIRST_EXPERT:
                    for name, value in zip(("lo_pool", "lo_dve"), mix_lo(4 * (n - NSLOT) + 3)):
                        sp.wait_ge(S[name], value)
                elif n >= FIRST_EXPERT:
                    sp.wait_ge(S["y_ready"], 2 * NT)
                sp.dma_start(ring[:, n % NSLOT, :].rearrange("p (k n) -> p k n", k=k), src).then_inc(ring_full[n % NSLOT], 16)

            for n in range(4):
                piece(n, ada_v[:, :, n * G:(n + 1) * G], KD)
            for g in WIN_ORDER:
                piece(WIN[g], win_v[:, :, WIN_COL[g] * G:(WIN_COL[g] + 1) * G], KD)
            for n in range(4, 12):
                piece(ADA[n], ada_v[:, :, n * G:(n + 1) * G], KD)
            for n in range(3):
                piece(WOUT[n], a["w_out"][0, n * G:(n + 1) * G, :].rearrange("(k p) n -> p k n", p=P), C)
            names = ("w_gate", "w_up", "w_down")
            for j in range(3):
                piece(FIRST_EXPERT + j, a[names[j]][0, 0].rearrange("(k p) n -> p k n", p=P), C if j == 2 else KD)

            def experts(first, start):
                with sp.Fori(start, NE) as i:
                    for j in range(3):
                        slot = (FIRST_EXPERT + j) % NSLOT
                        sp.wait_ge(S["unit_used"], 12 * i + (MIX_USED + 12 * (first - 1) + 4 * (j + 1)))
                        src = a[names[j]][0][bass.ds(i, 1)].rearrange("a (k p) n -> p (a k) n", p=P)
                        k = C if j == 2 else KD
                        sp.dma_start(ring[:, slot, :].rearrange("p (k n) -> p k n", k=k), src).then_inc(ring_full[slot], 16)

            experts(0, 1)
            sp.wait_ge(S["route_ready"], 1)
            over = sp.value_load(over_i[0:1, 0:1], min_val=0, max_val=T)
            with sp.If(over > P):
                experts(NE, 0)
                experts(2 * NE, 0)

        @block.gpsimd
        def _(pool):
            split = [0]

            def lo_to(last):
                while split[0] <= last:
                    u = split[0]
                    split[0] += 1
                    if u in DVE_MIX:
                        continue
                    pool.wait_ge(S["hi_ready"], u + 1)
                    col = BY_COLUMN[u]
                    raw, hi, lo = raw_unit(u // 4 % NSLOT, u % 4, col), part_unit(w_hi, u % 4, col), part_unit(w_lo, u % 4, col)
                    pool.tensor_tensor(lo, raw, hi.bitcast(F32), ALU.subtract).then_inc(S["lo_pool"], 1)

            pool.dma_start(ident, a["consts"][:, 0:128]).then_inc(S["consts_in"], 16)
            pool.dma_start(x_in[:, 0, :], a["x_prompt"][0]).then_inc(S["x_in"], 16)
            pool.dma_start(x_in[:, 1:3, :], a["x_sample"][0].rearrange("(i p) d -> p i d", p=P)).then_inc(S["x_in"], 16)
            pool.dma_start(pos_in, a["pos"].rearrange("(i p) d -> p i d", p=P)).then_inc(S["pos_in"], 16)
            pool.dma_start(gate_w, a["w_in"][0, :, GATE_OFF:D_IN].rearrange("(k p) n -> p k n", p=P)).then_inc(S["gate_w_in"], 16)
            pool.dma_start(gbias, a["b_in"][0, GATE_OFF:D_IN].partition_broadcast(P)).then_inc(S["gate_w_in"], 16)
            pool.dma_start(w_router, a["w_router"].rearrange("(k p) n -> p k n", p=P)).then_inc(S["mini_in"], 16)
            pool.dma_start(m0_rows[0:H, :], a["state_mlstm_m"][0, 0].rearrange("d h -> h d"), allow_slow_non_contiguous=True).then_inc(S["mini_in"], 16)
            pool.dma_start(m0_cols, a["state_mlstm_m"][0, 0].rearrange("d h -> (d h)").partition_broadcast(P)).then_inc(S["mini_in"], 16)
            pool.dma_start(masks_wide, a["hg_masks"]).then_inc(S["masks_in"], 16)
            lo_to(4 * 4 - 1)
            pool.memset(w_bd, 0.0).then_inc(S["lru_zeroed"], 1)
            pool.wait_ge(S["lru_zeroed"], 1)
            for d in range(2):
                for g, name in enumerate(("lru_wa", "lru_wx")):
                    for b in range(2):
                        src = a[name][0, d].rearrange("(c b) i e -> b i c e", b=2)[b]
                        pool.dma_start(w_bd[64 * b:64 * b + 64, d, g, :, 64 * b:64 * b + 64], src).then_inc(S["lru_w_in"], 16)

            pool.wait_ge(S["masks_in"], 16)
            pool.tensor_copy(hg_masks.rearrange("p d l t -> p (d l t)"), masks_wide).then_inc(S["masks_cast"], 1)
            lo_to(4 * WIN["gi"] + 3)

            def value_bias(n, g, dst, row):
                pool.dma_start(row, a["b_in"][0, WIN_COL[g] * G:(WIN_COL[g] + 1) * G].partition_broadcast(P)).then_inc(S["vbias_in"], 16)
                pool.wait_ge(S["vbias_in"], 16 * (n + 1))
                for i in range(NT):
                    pool.wait_ge(S["z_taken"], Z_INDEX[("tok", g)] + i + 1)
                    pool.tensor_tensor(dst[:, i, :], dst[:, i, :], row, ALU.add).then_inc(S["vbias_added"], 1)

            pool.wait_ge(S["pos_added"], 1)
            lo_to(4 * WIN["go"] + 3)
            value_bias(0, "gi", VH, unit(10, 0, G))
            lo_to(4 * WIN["mq"] + 3)
            pool.wait_ge(S["lru_done"], C)
            pool.dma_start(S0, a["state_hgrn_S"][0, 0].rearrange("d h p e -> p (d h) e")).then_inc(S["s0_in"], 16)
            lo_to(MIX_UNITS - 1)
            pool.wait_ge(S["hg_final"], 1)
            pool.dma_start(C0, a["state_mlstm_C"][0, 0].rearrange("d h p e -> p (d h) e")).then_inc(S["c0_in"], 16)
            pool.wait_ge(S["z_taken"], Z_COUNT)
            value_bias(1, "mv", MV, unit(6, 1024, G))
            pool.dma_start(outs[2][0, 0].rearrange("d (c p) -> p d c", p=P), h_fin, allow_slow_non_contiguous=True).then_inc(S["out_h"], 16)
            pool.wait_ge(S["s_fin_sb"], 8)
            pool.dma_start(outs[3][0, 0].rearrange("d h p e -> p (d h) e"), S_FIN).then_inc(S["out_S"], 16)
            pool.wait_ge(S["m_rows"], 1)
            pool.dma_start(outs[6][0, 0].rearrange("d h -> h d"), m_fin[0:H, :], allow_slow_non_contiguous=True).then_inc(S["out_m"], 16)
            for n in range(8):
                d = n % 2
                pool.wait_ge(S["p_exp"], n + 1)
                pool.wait_ge(S["ke_ready"], n + 1)
                v = PW_[:, n % 2, :].rearrange("p (b t) -> p b t", t=P)
                sgn = 1 - 2 * d
                for part, nb in ((v[:, 0:2, :], 2), (v[:, 3:4, :], 1)):
                    ins = pool.affine_select(out=part, in_=part, compare_op=ALU.is_ge, fill=0.0, base=0,
                                             pattern=[[0, nb], [sgn, P]], channel_multiplier=-sgn)
                    ins.then_inc(S["p_mask"], 1)
            pool.wait_ge(S["cfin_sb"], 16)
            pool.dma_start(outs[4][0, 0].rearrange("d h p e -> p (d h) e"), C_FIN).then_inc(S["out_C"], 16)
            pool.dma_start(outs[5][0, 0].rearrange("d h p -> p (d h)"), n_fin, allow_slow_non_contiguous=True).then_inc(S["out_n"], 16)
            pool.wait_ge(S["ml_done"], 1)
            pool.dma_start(X1[:, 0, :], a["x_prompt"][0]).then_inc(S["x2_in"], 16)
            pool.dma_start(X1[:, 1:3, :], a["x_sample"][0].rearrange("(i p) d -> p i d", p=P)).then_inc(S["x2_in"], 16)
            pool.dma_start(pos2, a["pos"].rearrange("(i p) d -> p i d", p=P)).then_inc(S["pos2_in"], 16)
            for v, name in enumerate(("ln1_g", "ln1_b", "ln2_g", "ln2_b")):
                pool.dma_start(ln_b[:, v, :], a[name][0].partition_broadcast(P)).then_inc(S["ln_in"], 16)
            pool.dma_start(b_router, a["b_router"].partition_broadcast(P)).then_inc(S["ln_in"], 16)
            pool.dma_start(tri, a["consts"][:, 128:256]).then_inc(S["ln_in"], 16)
            pool.dma_start(iota, a["consts"][:, 256:384]).then_inc(S["ln_in"], 16)
            pool.dma_start(desc16, a["consts"][:, 384:400]).then_inc(S["ln_in"], 16)
            pool.wait_ge(S["bcast_taken"], 16)
            pool.tensor_copy(g2_b, g2_made).then_inc(S["g2_moved"], 1)

            def expert_lo(n):
                for j in range(3):
                    for q in POOL_Q[j]:
                        pool.wait_ge(S["hi_ready"], 12 * n + (MIX_UNITS + 4 * j + q + 1))
                        raw = raw_unit((FIRST_EXPERT + j) % NSLOT, q, False)
                        pool.tensor_tensor(w_lo[:, q, :], raw, w_hi[:, q, :].bitcast(F32), ALU.subtract).then_inc(S["lo_pool"], 1)

            with pool.Fori(0, NE) as i:
                expert_lo(i)
            pool.wait_ge(S["route_ready"], 1)
            over = pool.value_load(over_i[0:1, 0:1], min_val=0, max_val=T)
            with pool.If(over > P):
                with pool.Fori(NE, 3 * NE) as i:
                    expert_lo(i)
            for i in range(NT):
                pool.wait_ge(S["out_tile"], i + 1)
                dst = outs[0][0] if i == 0 else outs[1][0, (i - 1) * P:i * P, :]
                pool.dma_start(dst, X1[:, i, :]).then_inc(S["out_y"], 16)
            pool.wait_ge(S["out_y"], 16 * NT)
            for n in ("out_h", "out_S", "out_C", "out_n", "out_m"):
                pool.wait_ge(S[n], 16)

        @block.scalar
        def _(act):
            done = {}

            def step(ins, name):
                done[name] = done.get(name, 0) + 1
                ins.then_inc(S[name], 1)
                act.wait_ge(S[name], done[name])

            bias_col = {g: A_BIN + 4 * WIN_COL[g] for g in WIN_COL}
            func = {"rx": ACT.Identity, "rg": ACT.Gelu_apprx_tanh, "gq": ACT.Silu, "gff": ACT.Sigmoid, "gfb": ACT.Sigmoid,
                    "go": ACT.Silu, "mq": ACT.Identity, "mk": ACT.Identity, "mo": ACT.Sigmoid}
            dst_of = {"rx": RX, "rg": YR, "gq": QFF, "gff": FF, "gfb": FB, "go": YH, "mq": MQ, "mk": MK, "mo": YM}

            def lru_gates(c):
                act.wait_ge(S["gates_ready"], c + 1)
                act.wait_ge(S["sp_ready"], 1)
                if c:
                    act.wait_ge(S["lru_done"], c)
                for d in range(2):
                    act.activation(R_[:, d * T:(d + 1) * T], ps[:, 4 + 2 * d, 0:T], ACT.Sigmoid,
                                   bias=colsB[:, B_BA + 4 * d + c:B_BA + 4 * d + c + 1]).then_inc(S["gates_taken"], 1)
                    act.activation(I_[:, d * T:(d + 1) * T], ps[:, 5 + 2 * d, 0:T], ACT.Sigmoid,
                                   bias=colsB[:, B_BX + 4 * d + c:B_BX + 4 * d + c + 1]).then_inc(S["gates_taken"], 1)
                act.wait_ge(S["gates_taken"], 4 * c + 4)
                for d in range(2):
                    k = 4 * d + c
                    step(act.activation(A_[:, d * T:(d + 1) * T], R_[:, d * T:(d + 1) * T], ACT.Exp, scale=nsp[:, k:k + 1]), "lru_act")
                for d in range(2):
                    k = 4 * d + c
                    step(act.activation(R_[:, d * T:(d + 1) * T], R_[:, d * T:(d + 1) * T], ACT.Tanh, scale=psp[:, k:k + 1]), "lru_act")

            def lru_sqrt(c):
                act.wait_ge(S["lru_den"], c + 1)
                act.activation(R_, R_, ACT.Sqrt, scale=2.0).then_inc(S["lru_sqrt"], 1)

            rounded = [0]

            def hi_to(last):
                while rounded[0] <= min(last, MIX_UNITS - 1):
                    u = rounded[0]
                    p = u // 4
                    act.wait_ge(ring_full[p % NSLOT], 16 * (p // NSLOT + 1))
                    if u >= 4:
                        act.wait_ge(S[USED[u - 4][0]], USED[u - 4][1])
                    col = BY_COLUMN[u]
                    act.activation(part_unit(w_hi, u % 4, col), raw_unit(p % NSLOT, u % 4, col), ACT.Copy).then_inc(S["hi_ready"], 1)
                    rounded[0] += 1

            for job in JOBS:
                kind = job[0]
                if kind == "lru":
                    lru_gates(job[1])
                    continue
                if kind == "lru2":
                    lru_sqrt(job[1])
                    continue
                if kind not in Z_KINDS:
                    continue
                n = Z_INDEX[job]
                bank = ps[:, n % 4, :]
                if kind == "gates":
                    act.wait_ge(S["h_ready"], 16)
                    act.activation(HH, hT, ACT.Copy).then_inc(S["h_hi"], 1)
                if kind in ("ada_row", "tok"):
                    hi_to(job_units(job)[-1] + 4)
                act.wait_ge(S["z_ready"], n + 1)
                if kind == "rows":
                    act.activation(colsA, bank[:, 0:A_ROWS], ACT.Identity).then_inc(S["cols_ready"], 1)
                    act.activation(colsB, bank[:, 128:128 + B_ROWS], ACT.Identity).then_inc(S["cols_ready"], 1)
                    act.wait_ge(S["cols_ready"], 2)
                    act.activation(silu_cols, colsB[:, B_C:B_C + 16], ACT.Silu).then_inc(S["z_taken"], 1)
                    act.wait_ge(S["z_taken"], 1)
                    act.activation(silu_hi, silu_cols, ACT.Copy).then_inc(S["silu_c"], 1)
                elif kind == "xT":
                    _, i, half = job
                    act.activation(hT[:, 4 * half:4 * half + 4, i * P:(i + 1) * P], bank.rearrange("p (k t) -> p k t", k=4),
                                   ACT.Identity).then_inc(S["z_taken"], 1)
                    if (i, half) == (NT - 1, 1):
                        act.wait_ge(S["lb_diff"], 1)
                        act.activation(tiny_tmp[:, 0:8], tiny_tmp[:, 0:8], ACT.Exp).then_inc(S["lb_exp"], 1)
                        act.wait_ge(S["lam_abs"], 1)
                        act.activation(nsp, nsp, ACT.Exp, scale=-1.0).then_inc(S["lam_exp"], 1)
                elif kind == "ada_row":
                    act.activation(ada_rows[0:2, job[1] % 2, :], bank[0:2, :], ACT.Identity).then_inc(S["z_taken"], 1)
                elif kind == "ada_col":
                    act.activation(modc[:, 4 * job[1]:4 * job[1] + 4, :], bank[:, 0:8].rearrange("p (c s) -> p c s", s=2),
                                   ACT.Identity).then_inc(S["z_taken"], 1)
                elif kind == "tok":
                    g = job[1]
                    if g == "mv":
                        act.wait_ge(S["vbias_added"], NT)
                    for i in range(NT):
                        act.activation((VH if g == "gi" else MV)[:, i, :], ps[:, (n + i) % 4, :], ACT.Identity).then_inc(S["z_taken"], 1)
                elif kind == "gates":
                    act.activation(gz, bank[:, 0:48].rearrange("p (i g) -> p i g", i=NT), ACT.Identity).then_inc(S["z_taken"], 1)
                else:
                    _, g, c = job
                    bias = colsA[:, bias_col[g] + c:bias_col[g] + c + 1]
                    if g == "go" and c == 0:
                        act.wait_ge(S["masks_cast"], 1)
                    if g == "mk":
                        act.wait_ge(S["sp_ready"], 1)
                        act.activation(chunk(MK, c), bank[:, 0:T], ACT.Identity, bias=tiny_tmp[:, 28 + c:29 + c], scale=KSCALE).then_inc(S["z_taken"], 1)
                    else:
                        act.activation(chunk(dst_of[g], c), bank[:, 0:T], func[g], bias=bias).then_inc(S["z_taken"], 1)
                    hi_to(job_units(job)[0] + 4)

            for d in range(2):
                act.wait_ge(S["gz_rows_T"], 2 * d + 1)
                act.activation(GI[:, d, :], ps[0:H, 2 * d, 0:T], ACT.Identity).then_inc(S["gz_rows"], 1)
                act.wait_ge(S["gz_rows_T"], 2 * d + 2)
                act.activation(GF[:, d, :], ps[0:H, 2 * d + 1, 0:T], ACT.Identity).then_inc(S["gz_rows"], 1)
            def broadcast_rows(jobs):
                for n in jobs:
                    v, s, half = n // 4, (n // 2) % 2, n % 2
                    dst = (g1_b, sh2_b, sc2_b, g2_made)[v][:, s, half * 512:(half + 1) * 512]
                    act.wait_ge(S["bcast_ready"], n + 1)
                    act.activation(dst, ps[:, 4 + n % 4, :], ACT.Identity,
                                   bias=1.0 if v == 2 else 0.0).then_inc(S["bcast_taken"], 1)

            for n in range(8):
                act.wait_ge(S["kb_T"], n + 1)
                if n == 0:
                    act.wait_ge(S["hg_final"], 1)
                if n >= 4:
                    act.wait_ge(S["s_fin"], n - 3)
                act.activation(KB_T[:, n % 4, :], ps[:, n % 2, 0:P], ACT.Identity).then_inc(S["kb_T_sb"], 1)
                if n >= 1:
                    act.wait_ge(S["s_fin"], n)
                    act.activation(S_FIN[:, n - 1, :], ps[:, 2 + (n - 1) % 2, 0:P], ACT.Identity).then_inc(S["s_fin_sb"], 1)
                broadcast_rows((2 * n, 2 * n + 1))
                if n == 3:
                    act.wait_ge(S["f_abs"], 1)
                    act.activation(FE, FE, ACT.Exp, scale=-1.0).then_inc(S["f_exp"], 1)
                    act.wait_ge(S["f_exp"], 1)
                    act.activation(FE, FE, ACT.Ln, bias=1.0).then_inc(S["f_ln"], 1)
            act.wait_ge(S["s_fin"], 8)
            act.activation(S_FIN[:, 7, :], ps[:, 3, 0:P], ACT.Identity).then_inc(S["s_fin_sb"], 1)
            for h in range(H + 1):
                if h < H:
                    act.wait_ge(S["o_ready"], h + 1)
                    if h >= 2:
                        act.wait_ge(S["o_var"], h - 1)
                    act.activation(O_SQ[:, h % 2, :], ps[:, 4 + h, 0:T], ACT.Square).then_inc(S["o_sq"], 1)
                if h == 1:
                    act.wait_ge(S["c_T"], 1)
                    act.activation(c_cols.rearrange("p d i h -> p (d i h)"), ps[:, 0, 0:24], ACT.Identity).then_inc(S["c_cols"], 1)
                    act.wait_ge(S["kT_ready"], 1)
                    act.activation(KTOK, ps[:, 1, :], ACT.Identity).then_inc(S["kT_sb"], 1)
                if h >= 1:
                    act.wait_ge(S["o_var"], h)
                    if h >= 3:
                        act.wait_ge(S["o_norm"], h - 2)
                    act.activation(O_STD[:, (h - 1) % 2, :], ps[:, 2 + (h - 1) % 2, 0:T], ACT.Sqrt, bias=eps).then_inc(S["o_std"], 1)


            def weights_of(n):
                h, d, b = n // 2, n % 2, n % 2
                act.wait_ge(S["bc_ready"], n + 1)
                if n >= 2:
                    act.wait_ge(S["qs_ready"], n - 1)
                act.activation(SI[:, b, :], ps[:, 0, SEQ:T], ACT.Exp, scale=-1.0,
                               bias=m0_cols[:, 4 * d + h:4 * d + h + 1]).then_inc(S["si_ready"], 1)
                if n >= 2:
                    act.wait_ge(S["h_done"], n - 1)
                act.activation(FLOOR[:, b, :], ps[:, 1, 0:T], ACT.Exp).then_inc(S["den_floor"], 1)
                act.wait_ge(S["p_arg"], n + 1)
                act.activation(PW_[:, b, :], PW_[:, b, :], ACT.Exp, scale=-1.0).then_inc(S["p_exp"], 1)

            weights_of(0)
            for n in range(9):
                h, d = n // 2, n % 2
                if n < 7:
                    weights_of(n + 1)
                if n < 8:
                    act.wait_ge(S["cfin_ready"], n + 1)
                    act.activation(C_FIN[:, 4 * d + h, :], ps[:, 3, 0:P], ACT.Identity).then_inc(S["cfin_sb"], 1)
                    act.activation(n_fin[:, 4 * d + h:4 * d + h + 1], ps[:, 3, 128:129], ACT.Identity).then_inc(S["cfin_sb"], 1)
                if d == 0 and n:
                    act.wait_ge(S["hc_ready"], h)
                    act.activation(HT2[:, 1, :], HT2[:, 0, :], ACT.Square).then_inc(S["hsq_ready"], 1)
                if n < 8:
                    act.wait_ge(S["num_ready"], n + 1)
                    act.activation(DEN[:, n % 2, :], ps[:, 5, 0:T], ACT.Abs).then_inc(S["den_abs"], 1)
                if d == 0 and n:
                    act.wait_ge(S["hv_ready"], h)
                    act.activation(HT2[:, 1, :], ps[:, 7, 0:T], ACT.Sqrt, bias=eps).then_inc(S["hstd_ready"], 1)

            def split_rows(i):
                act.wait_ge(S["ln_var"], i + 1)
                act.activation(rstd, mv_stats[:, 13:14], ACT.Sqrt, bias=eps).then_inc(S["ln_std"], 1)
                act.wait_ge(S["h2_ready"], i + 1)
                act.activation(H2H[:, i, :], H2[:, i, :], ACT.Copy).then_inc(S["h2_hi"], 1)

            def turned_rows(i):
                for half in range(2):
                    act.wait_ge(S["h2_T"], 2 * i + half + 1)
                    act.activation(h2T[:, 4 * half:4 * half + 4, :], ps[:, 6 + half, :].rearrange("p (k t) -> p k t", k=4),
                                   ACT.Identity).then_inc(S["h2_T_sb"], 1)

            for i in range(NT - 1):
                split_rows(i)
            for i in range(NT - 1):
                turned_rows(i)
            split_rows(NT - 1)
            turned_rows(NT - 1)
            act.wait_ge(S["smax_ready"], 1)
            act.activation(scores, scores, ACT.Exp).then_inc(S["sexp_ready"], 1)

            def gather_rows(n, half):
                act.wait_ge(S["g_rows"], 2 * n + (half + 1))
                act.activation(GT[:, half, :], ps[:, half, :], ACT.Identity).then_inc(S["g_rows_sb"], 1)

            def gather_slots(n, b):
                act.wait_ge(S["gathered"], n + 1)
                act.activation(slot_w, ps[:, 2, T:T + 1], ACT.Identity)
                act.activation(SelT[:, b, :], ps[:, 2, 0:T], ACT.Copy).then_inc(S["gather_taken"], 1)

            def gather_hi(n):
                for half in range(2):
                    act.wait_ge(S["g_rows_T"], 2 * n + (half + 1))
                    act.activation(HGH[:, 4 * half:4 * half + 4, :], ps[:, half, :].rearrange("p (k j) -> p k j", k=4),
                                   ACT.Copy).then_inc(S["gather_taken"], 1)

            def expert_hi(n, j, quarters=range(4)):
                slot = (FIRST_EXPERT + j) % NSLOT
                act.wait_ge(ring_full[slot], 16 * n + 16 * ((FIRST_EXPERT + j) // NSLOT + 1))
                for q in quarters:
                    act.wait_ge(S["unit_used"], 12 * n + (MIX_USED + 4 * j + q - 3))
                    act.activation(w_hi[:, q, :], raw_unit(slot, q, False), ACT.Copy).then_inc(S["hi_ready"], 1)

            def expert(n, b, more):
                expert_hi(n, 1)
                act.wait_ge(S["unit_used"], 12 * n + (MIX_USED + 4))
                act.activation(SG, ps[:, 3, :], ACT.Silu).then_inc(S["sg_ready"], 1)
                expert_hi(n, 2)
                if more:
                    gather_rows(n + 1, 0)
                act.wait_ge(S["act_T"], n + 1)
                act.activation(ACH, ps[:, 3, :].rearrange("p (k j) -> p k j", k=C), ACT.Copy).then_inc(S["act_T_sb"], 1)
                if more:
                    gather_rows(n + 1, 1)
                    gather_slots(n + 1, 1 - b)
                    expert_hi(n + 1, 0, (0,))
                    gather_hi(n + 1)
                    expert_hi(n + 1, 0, (1, 2, 3))
                act.wait_ge(S["unit_used"], 12 * n + (MIX_USED + 12))
                for half in range(2):
                    act.activation(DNH[:, half, :], ps[:, 5 + half, :], ACT.Copy).then_inc(S["down_sb"], 1)

            def expert_pass(base):
                expert_hi(base, 0)
                for half in range(2):
                    gather_rows(base, half)
                gather_slots(base, 0)
                gather_hi(base)
                expert(base, 0, True)
                with act.Fori(0, NPAIR - 1) as i:
                    expert(2 * i + (base + 1), 1, True)
                    expert(2 * i + (base + 2), 0, True)
                expert(base + NE - 1, 1, False)

            act.wait_ge(S["out_C"], 16)
            act.wait_ge(S["out_S"], 16)
            act.wait_ge(S["g2_moved"], 1)
            expert_pass(0)
            act.wait_ge(S["route_ready"], 1)
            over = act.value_load(over_i[0:1, 0:1], min_val=0, max_val=T)
            with act.If(over > P):
                expert_pass(NE)
                expert_pass(2 * NE)
            for i in range(NT):
                act.wait_ge(S["ln2_var"], i + 1)
                act.activation(rstd, mv_stats[:, 13:14], ACT.Sqrt, bias=eps).then_inc(S["ln2_std"], 1)

        @block.tensor
        def _(pe):
            def mm(out, lhsT, rhs, start=True, stop=True, open_=False):
                return pe.matmul(out, lhsT, rhs, start=start, stop=stop, skip_group_check=open_)

            def slot(n, k):
                return ring[:, n % NSLOT, :].rearrange("p (k n) -> p k n", k=k)

            def full(n):
                pe.wait_ge(ring_full[n % NSLOT], 16 * (n // NSLOT + 1))

            def mm3(out, lhsT, rhs, first, last):
                mm(out, lhsT[1], rhs[0], first, False)
                mm(out, lhsT[0], rhs[1], False, False)
                return mm(out, lhsT[0], rhs[0], False, last)

            def weights(u):
                if u in DVE_MIX:
                    pe.wait_ge(S["lo_dve"], mix_lo(u)[1])
                else:
                    pe.wait_ge(S["lo_pool"], mix_lo(u)[0])
                return [part_unit(x, u % 4, BY_COLUMN[u]) for x in (w_hi, w_lo)]

            def lru(c):
                if c == 0:
                    pe.wait_ge(S["lru_w_in"], 16 * 8)
                    pe.wait_ge(S["rx_conv"], 1)
                else:
                    pe.wait_ge(S["gates_taken"], 4 * c)
                for d in range(2):
                    for g in range(2):
                        last = mm(ps[:, 4 + 2 * d + g, 0:T], w_bd[:, d, g, c, :], chunk(XC, c))
                last.then_inc(S["gates_ready"], 1)

            hg_job = [0]

            def hg_bank():
                m = hg_job[0]
                hg_job[0] += 1
                if m >= 4:
                    pe.wait_ge(S["hg_taken"], m - 3)
                return ps[:, 4 + m % 4, :].rearrange("p (h t) -> p h t", h=H)

            def hg_mul(out, k, q, s, t, start=True, stop=True):
                return mm(out, k[:, s:s + P], q[:, t:t + P], start, stop)

            def hg_diag():
                pe.wait_ge(S["gates_taken"], 4 * C)
                pe.wait_ge(S["hg_start"], 1)
                for i in range(NT):
                    out = hg_bank()
                    for h in range(H):
                        hg_mul(out[:, h, :], chunk(KBF, h), chunk(QFF, h), i * P, i * P, True, False)
                        last = hg_mul(out[:, h, :], chunk(KBB, h), chunk(QFF, h), i * P, i * P, False, True)
                    last.then_inc(S["hg_scores"], 1)

            def hg_level(lv):
                pe.wait_ge(S["hg_level"], lv + 1)
                if lv < LEVELS:
                    todo = [(d, i * P, i * P) for i in range(NT) for d in range(2)]
                else:
                    todo = [(0, P, 2 * P), (1, 2 * P, P)]
                for d, s, t in todo:
                    out = hg_bank()
                    for h in range(H):
                        last = hg_mul(out[:, h, :], chunk((KBF, KBB)[d], h), chunk((QFF, QFB)[d], h), s, t)
                    last.then_inc(S["hg_scores"], 1)

            for job in JOBS:
                kind = job[0]
                if kind == "lru":
                    lru(job[1])
                    continue
                if kind == "hg_diag":
                    hg_diag()
                    continue
                if kind == "hg_level":
                    hg_level(job[1])
                    continue
                if kind not in Z_KINDS:
                    continue
                n = Z_INDEX[job]
                bank = ps[:, n % 4, :]
                width = NT if kind == "tok" else 1
                if n + width > 4:
                    pe.wait_ge(S["z_taken"], n + width - 4)
                if kind == "rows":
                    pe.wait_ge(S["consts_in"], 16)
                    pe.wait_ge(S["rows_in"], 16 * 14)
                    pe.transpose(bank[:, 0:A_ROWS], rowsA[0:A_ROWS, :], ident[0:A_ROWS, 0:A_ROWS])
                    last = pe.transpose(bank[:, 128:128 + B_ROWS], rowsB[0:B_ROWS, :], ident[0:B_ROWS, 0:B_ROWS])
                elif kind == "xT":
                    _, i, half = job
                    if i == 0 and half == 0:
                        pe.wait_ge(S["x_in"], 32)
                    if i == 1 and half == 0:
                        pe.wait_ge(S["pos_added"], 1)
                    for k in range(4):
                        last = pe.transpose(bank[:, k * P:(k + 1) * P], x_in[:, i, (4 * half + k) * P:(4 * half + k + 1) * P], ident)
                elif kind == "ada_row":
                    pe.wait_ge(S["silu_c2"], 1)
                    for q, u in enumerate(job_units(job)):
                        w = weights(u)
                        for kk in range(2):
                            k = 2 * q + kk
                            last = mm3(bank[0:2, :], [x[:, k:k + 9:8] for x in (silu_hi, silu_lo)],
                                       [x[:, kk * G:(kk + 1) * G] for x in w], k == 0, k == KD - 1)
                        if q < 3:
                            last.then_inc(S["unit_used"], 1)
                elif kind == "ada_col":
                    pe.wait_ge(S["z_taken"], Z_INDEX[("ada_row", job[1])] + 1)
                    for c in range(4):
                        last = mm(bank[:, 2 * c:2 * c + 2], ada_rows[0:2, job[1] % 2, c * P:(c + 1) * P], ident[0:2, 0:2])
                elif kind == "tok":
                    for q, u in enumerate(job_units(job)):
                        w = weights(u)
                        for i in range(NT):
                            for kk in range(2):
                                k = 2 * q + kk
                                last = mm3(ps[:, (n + i) % 4, :], [x[:, k, i * P:(i + 1) * P] for x in (HH, HL)],
                                           [x[:, kk * G:(kk + 1) * G] for x in w], k == 0, k == KD - 1)
                        if q < 3:
                            last.then_inc(S["unit_used"], 1)
                elif kind == "gates":
                    pe.wait_ge(S["gate_w_in"], 32)
                    pe.wait_ge(S["h_ready"], 16)
                    for i in range(NT):
                        for k in range(KD):
                            last = mm(bank[:, 16 * i:16 * i + 16], hT[:, k, i * P:(i + 1) * P], gate_w[:, k, :], k == 0, k == KD - 1)
                else:
                    _, g, c = job
                    if g == "rx":
                        pe.wait_ge(S["h_lo"], 1)
                    w = weights(job_units(job)[0])
                    for k in range(KD):
                        last = mm3(bank[:, 0:T], [x[:, k, :] for x in w], [x[:, k, :] for x in (HH, HL)], k == 0, k == KD - 1)
                last.then_inc(S["z_ready"], width)

            pe.wait_ge(S["z_taken"], Z_COUNT)
            pe.wait_ge(S["gz_ready"], 1)
            for d in range(2):
                for ty in range(2):
                    for i in range(NT):
                        last = pe.transpose(ps[0:H, 2 * d + ty, i * P:(i + 1) * P], gz[:, i, 8 * d + 4 * ty:8 * d + 4 * ty + 4], ident)
                    last.then_inc(S["gz_rows_T"], 1)
            def broadcast_rows(jobs):
                for n in jobs:
                    v, s, half = n // 4, (n // 2) % 2, n % 2
                    if n >= 4:
                        pe.wait_ge(S["bcast_taken"], n - 3)
                    for k in range(4):
                        col = modc[:, 8 * (G1, SH2, SC2, G2)[v] + 4 * half + k, s:s + 1].broadcast_to([P, P])
                        last = mm(ps[:, 4 + n % 4, k * P:(k + 1) * P], col, ident)
                    last.then_inc(S["bcast_ready"], 1)

            pe.wait_ge(S["gz_rows"], 4)
            pe.wait_ge(S["vbias_added"], NT)
            pe.wait_ge(S["hg_taken"], hg_job[0])
            pe.wait_ge(S["mod2_ready"], 1)
            for n in range(8):
                d, h = n // 4, n % 4
                if n >= 2:
                    pe.wait_ge(S["kb_T_sb"], n - 1)
                pe.transpose(ps[:, n % 2, 0:P], chunk((KBF, KBB)[d], h)[:, 0:P], ident).then_inc(S["kb_T"], 1)
                broadcast_rows((2 * n, 2 * n + 1))
                pe.wait_ge(S["kb_T_sb"], n + 1)
                if n >= 2:
                    pe.wait_ge(S["s_fin_sb"], n - 1)
                mm(ps[:, 2 + n % 2, 0:P], KB_T[:, n % 4, :], VH[:, 0, h * P:(h + 1) * P]).then_inc(S["s_fin"], 1)
            pe.wait_ge(S["s0_in"], 16)
            pe.wait_ge(S["hg_final"], 1)
            pe.wait_ge(S["bcast_taken"], 16)

            def o_var(h):
                pe.wait_ge(S["o_sq"], h + 1)
                if h >= 2:
                    pe.wait_ge(S["o_std"], h - 1)
                mm(ps[:, 2 + h % 2, 0:T], mean_w, O_SQ[:, h % 2, :]).then_inc(S["o_var"], 1)

            pe.wait_ge(S["s_fin_sb"], 8)
            for h in range(H):
                o = ps[:, 4 + h, 0:T]
                v = [VH[:, i, h * P:(h + 1) * P] for i in range(NT)]
                mm(o[:, 0:P], v[0], SCO[:, 0, h, :])
                mm(o[:, SEQ:T], S0[:, h, :], chunk(QFF, h)[:, SEQ:T], True, False)
                mm(o[:, P:2 * P], v[1], SCO[:, 1, h, :], False, False, True)
                mm(o[:, P:2 * P], v[2], SCX[:, 1, h, :], False, False, True)
                mm(o[:, 2 * P:T], v[2], SCO[:, 2, h, :], False, False, True)
                mm(o[:, 2 * P:T], v[1], SCX[:, 0, h, :], False, False, True)
                mm(o[:, SEQ:T], S0[:, 4 + h, :], chunk(QFB, h)[:, SEQ:T], False, True).then_inc(S["o_ready"], 1)
                if h == 1:
                    pe.wait_ge(S["m_rows"], 1)
                    for d in range(2):
                        for i in range(NT):
                            at_ = 12 * d + 4 * i
                            last = pe.transpose(ps[:, 0, at_:at_ + 4], CR[:, d, i * P:(i + 1) * P], ident[0:H, 0:H])
                    last.then_inc(S["c_T"], 1)
                    for x in range(H):
                        last = pe.transpose(ps[:, 1, x * P:(x + 1) * P], chunk(MK, x)[:, 0:P], ident)
                    last.then_inc(S["kT_ready"], 1)
                if h >= 1:
                    o_var(h - 1)
            o_var(H - 1)

            pe.wait_ge(S["c_cols"], 1)
            pe.wait_ge(S["kT_sb"], 1)
            pe.wait_ge(S["vbias_added"], 2 * NT)
            pe.wait_ge(S["c0_in"], 16)

            def rows_of(n):
                h, d = n // 2, n % 2
                pick = ident[0:H, h:h + 1].broadcast_to([H, P])
                if n >= 1:
                    pe.wait_ge(S["p_arg"], n)
                    pe.wait_ge(S["den_floor"], n)
                mm(ps[:, 0, 0:T], pick, MR[:, d, :])
                mm(ps[:, 1, 0:T], pick, NBM[:, d, :]).then_inc(S["bc_ready"], 1)

            def scores_of(n):
                h, d = n // 2, n % 2
                q, k = chunk(MQ, h), chunk(MK, h)
                if n >= 1:
                    pe.wait_ge(S["w_ready"], n)
                mm(ps[:, 2, 0:P], k[:, 0:P], q[:, 0:P])
                if d == 0:
                    mm(ps[:, 2, P:3 * P], k[:, P:2 * P], q[:, P:T])
                    last = mm(ps[:, 2, 3 * P:4 * P], k[:, 2 * P:T], q[:, 2 * P:T])
                else:
                    mm(ps[:, 2, P:2 * P], k[:, P:2 * P], q[:, P:2 * P])
                    last = mm(ps[:, 2, 2 * P:4 * P], k[:, 2 * P:T], q[:, P:T])
                last.then_inc(S["ml_scores"], 1)

            def project(i, half, parts):
                for kk in parts:
                    y = (YR, YH, YM)[kk // 4]
                    last = mm(ps[:, 2 * i + half, :], chunk(y, kk % 4)[:, i * P:(i + 1) * P],
                              slot(WOUT[kk // 4], C)[:, kk % 4, half * 512:(half + 1) * 512], kk == 0, kk == 11)
                return last

            rows_of(0)
            pe.wait_ge(S["o_std"], H)
            scores_of(0)
            for n in range(9):
                h, d = n // 2, n % 2
                b = n % 2
                if n < 7:
                    rows_of(n + 1)
                if n < 8:
                    pe.wait_ge(S["ke_ready"], n + 1)
                    if n >= 1:
                        pe.wait_ge(S["cfin_sb"], 2 * n)
                    v = [MV[:, i, h * P:(h + 1) * P] for i in range(NT)]
                    mm(ps[:, 3, 0:P], KE[:, b, :], v[0])
                    mm(ps[:, 3, 128:129], KE[:, b, :], ones[:, 0:1]).then_inc(S["cfin_ready"], 1)
                if n < 7:
                    scores_of(n + 1)
                if n >= 1:
                    pe.wait_ge(S["h_done"], n)
                if d == 0 and n:
                    mm(ps[:, 6, 0:T], mean_w, HS[:, 1, :]).then_inc(S["hm_ready"], 1)
                if n < 8:
                    if n == 0:
                        pe.wait_ge(S["o_norm"], H)
                    pe.wait_ge(S["qs_ready"], n + 1)
                    pe.wait_ge(S["w_ready"], n + 1)
                    w = WW[:, b, :]
                    n0 = colsB[:, B_N0 + 4 * d + h:B_N0 + 4 * d + h + 1].broadcast_to([P, P])
                    for bank, c0, vs in ((4, C0[:, 4 * d + h, :], v), (5, n0, [ones] * NT)):
                        o = ps[:, bank, 0:T]
                        mm(o[:, 0:P], vs[0], w[:, 0:P])
                        mm(o[:, SEQ:T], c0, QS[:, b, :], True, False)
                        if d == 0:
                            mm(o[:, 2 * P:T], vs[2], w[:, 3 * P:4 * P], False, False, True)
                            last = mm(o[:, SEQ:T], vs[1], w[:, P:3 * P], False, True)
                        else:
                            mm(o[:, P:2 * P], vs[1], w[:, P:2 * P], False, False, True)
                            last = mm(o[:, SEQ:T], vs[2], w[:, 2 * P:4 * P], False, True)
                    last.then_inc(S["num_ready"], 1)
                if d == 0 and n:
                    if n == 8:
                        project(0, 1, range(0, 4))
                    pe.wait_ge(S["hsq_ready"], h)
                    mm(ps[:, 7, 0:T], mean_w, HT2[:, 1, :]).then_inc(S["hv_ready"], 1)
                if n == 7:
                    for m in WOUT:
                        full(m)
                    pe.wait_ge(S["p_arg"], 8)
                    pe.wait_ge(S["den_floor"], 8)
                    project(0, 0, range(0, 8))
            project(0, 1, range(4, 8))

            pe.wait_ge(S["ml_done"], 1)
            for i in range(NT):
                for half in range(2):
                    project(i, half, range(8 if i == 0 else 0, 12)).then_inc(S["y_ready"], 1)

            pe.wait_ge(S["mini_in"], 48)
            for i in range(NT):
                pe.wait_ge(S["h2_ready"], i + 1)
                for half in range(2):
                    if i:
                        pe.wait_ge(S["h2_T_sb"], 2 * i)
                    for k in range(4):
                        last = pe.transpose(ps[:, 6 + half, k * P:(k + 1) * P], H2[:, i, (4 * half + k) * P:(4 * half + k + 1) * P], ident)
                    last.then_inc(S["h2_T"], 1)
                pe.wait_ge(S["h2_T_sb"], 2 * i + 2)
                for k in range(KD):
                    last = mm(ps[:, 0, 16 * i:16 * i + 16], h2T[:, k, :], w_router[:, k, :], k == 0, k == KD - 1)
            last.then_inc(S["logits_ready"], 1)
            pe.wait_ge(S["mask_ready"], 1)
            pe.wait_ge(S["ln_in"], 16 * 8)
            for i in range(NT):
                for j in range(i + 1):
                    mm(ps[:, 1, 16 * i:16 * i + 16], tri if j == i else ones, mask[:, j, :], j == 0, j == i)
            for j in range(NT):
                last = mm(ps[:, 1, 48:64], ones, mask[:, j, :], j == 0, j == NT - 1)
            last.then_inc(S["ranks_ready"], 1)

            def gather_rows(n, half):
                pe.wait_ge(S["sel_ready"], n + 1)
                for i in range(NT):
                    for x in (H2L, H2H):
                        last = mm(ps[:, half, :], Sel[:, i, :], x[:, i, half * 512:(half + 1) * 512],
                                  i == 0 and x is H2L, i == NT - 1 and x is H2H)
                last.then_inc(S["g_rows"], 1)

            def gather_slots(n, wait_y=True):
                if wait_y:
                    pe.wait_ge(S["y_added"], 6 * n - 6)
                for i in range(NT):
                    pe.transpose(ps[:, 2, i * P:(i + 1) * P], Sel[:, i, :].bitcast(F32), ident)
                for i in range(NT):
                    last = mm(ps[:, 2, T:T + 1], Sel[:, i, :].bitcast(F32), pw[:, i, 1:2], i == 0, i == NT - 1)
                last.then_inc(S["gathered"], 1)

            def gather_turn(n):
                for half in range(2):
                    pe.wait_ge(S["g_rows_sb"], 2 * n + (half + 1))
                    for k in range(4):
                        last = pe.transpose(ps[:, half, k * P:(k + 1) * P], GT[:, half, k * P:(k + 1) * P], ident)
                    last.then_inc(S["g_rows_T"], 1)

            def expert_weights(n, j, q):
                if q in POOL_Q[j]:
                    pe.wait_ge(S["lo_pool"], POOL_N * n + (MIX_POOL + lo_counts(j, q)[0] + 1))
                else:
                    pe.wait_ge(S["lo_dve"], DVE_N * n + (MIX_DVE + lo_counts(j, q)[1] + 1))
                return [x[:, q, :] for x in (w_hi, w_lo)]

            def gate_up(n, before=None):
                pe.wait_ge(S["hg_lo"], 2 * n + 2)
                pe.wait_ge(S["gather_taken"], 3 * n + 3)
                for j, bank in ((0, 3), (1, 4)):
                    for q in range(4):
                        w = expert_weights(n, j, q)
                        for kk in range(2):
                            k = 2 * q + kk
                            last = mm3(ps[:, bank, :], [x[:, k, :] for x in (HGH, HGL)], [x[:, kk * G:(kk + 1) * G] for x in w],
                                       k == 0, k == KD - 1)
                        last.then_inc(S["unit_used"], 1)
                        if j == 1 and q < 3 and before is not None:
                            scatter(n - 1, before, (2 * q, 2 * q + 1))

            def act_transpose(n):
                pe.wait_ge(S["act_ready"], n + 1)
                for k in range(C):
                    last = pe.transpose(ps[:, 3, k * P:(k + 1) * P], AC[:, k * P:(k + 1) * P], ident)
                last.then_inc(S["act_T"], 1)

            def scatter(n, b, parts, last_of_pass=False):
                pe.wait_ge(S["down_lo"], 2 * n + 2)
                for r in parts:
                    i, half = r // 2, r % 2
                    if r >= 2 or last_of_pass:
                        pe.wait_ge(S["y_added"], 6 * n + (r - 1))
                    for x in (DNL, DNH):
                        last = mm(ps[:, (7, 2)[r % 2], :], SelT[:, b, i * P:(i + 1) * P], x[:, half, :], x is DNL, x is DNH)
                    last.then_inc(S["scattered"], 1)

            def down(n, quarters=range(4)):
                pe.wait_ge(S["act_lo"], n + 1)
                for q in quarters:
                    w = expert_weights(n, 2, q)
                    for half in range(2):
                        last = mm3(ps[:, 5 + half, :], [x[:, q, :] for x in (ACH, ACL)], [x[:, half * G:(half + 1) * G] for x in w],
                                   q == 0, q == 3)
                    last.then_inc(S["unit_used"], 1)

            def expert(n, before, wait_y=True):
                gate_up(n, before)
                gather_rows(n + 1, 0)
                act_transpose(n)
                gather_rows(n + 1, 1)
                gather_slots(n + 1, wait_y)
                down(n, (0,))
                gather_turn(n + 1)
                down(n, (1, 2, 3))

            def expert_pass(base):
                for half in range(2):
                    gather_rows(base, half)
                gather_slots(base, base > 0)
                gather_turn(base)
                if base:
                    pe.wait_ge(S["y_added"], 6 * base)
                expert(base, None, base > 0)
                with pe.Fori(0, NPAIR - 1) as i:
                    for m in (1, 2):
                        expert(2 * i + (base + m), 1 - m % 2)
                n = base + NE - 1
                gate_up(n, 0)
                act_transpose(n)
                down(n)
                scatter(n, 1, range(6), True)

            pe.wait_ge(S["route_ready"], 1)
            pe.wait_ge(S["h2_lo"], NT)
            expert_pass(0)
            over = pe.value_load(over_i[0:1, 0:1], min_val=0, max_val=T)
            with pe.If(over > P):
                expert_pass(NE)
                expert_pass(2 * NE)

        @block.vector
        def _(dve):
            done = {}

            def step(ins, name="dve"):
                done[name] = done.get(name, 0) + 1
                ins.then_inc(S[name], 1)
                dve.wait_ge(S[name], done[name])

            tt, ts, stt = dve.tensor_tensor, dve.tensor_scalar, dve.scalar_tensor_tensor
            mix_todo = list(DVE_MIX)

            def mix_lo_to(last, most=MIX_UNITS):
                while mix_todo and mix_todo[0] <= last and most > 0:
                    u = mix_todo.pop(0)
                    most -= 1
                    dve.wait_ge(S["hi_ready"], u + 1)
                    tt(w_lo[:, u % 4, :], raw_unit(u // 4 % NSLOT, u % 4, False), w_hi[:, u % 4, :].bitcast(F32),
                       ALU.subtract).then_inc(S["lo_dve"], 1)

            step(dve.memset(ones, 1.0))
            step(dve.memset(mean_w, 1.0 / P))
            step(dve.memset(eps, EPS))
            step(dve.memset(zeros4, 0.0))
            dve.wait_ge(S["x_in"], 32)
            dve.wait_ge(S["pos_in"], 16)
            step(tt(x_in[:, 1:3, :], x_in[:, 1:3, :], pos_in, ALU.add), "pos_added")

            dve.wait_ge(S["z_taken"], 1)
            dve.wait_ge(S["silu_c"], 1)
            step(tt(silu_lo, silu_cols, silu_hi.bitcast(F32), ALU.subtract), "silu_c2")
            mix_lo_to(3)
            raw = colsB[:, B_LB:B_LB + 8]
            t = [tiny_tmp[:, 8 * n:8 * n + 8] for n in range(3)]
            lam = colsB[:, B_LAM:B_LAM + 8]
            step(tt(t[0], raw, raw, ALU.subtract), "lb_diff")
            step(stt(nsp, lam, -1.0, lam, ALU.mult, ALU.max), "lam_abs")
            dve.wait_ge(S["lb_exp"], 1)
            step(dve.reciprocal(t[1], t[0]))
            step(tt(t[0], t[0], t[1], ALU.mult))
            step(tt(lb, t[0], t[0], ALU.subtract))
            step(ts(om_lb, lb, -1.0, 1.0, ALU.mult, ALU.add))
            step(ts(neg_om_lb, om_lb, -1.0, None, ALU.mult))
            for c in range(C):
                k = A_BIN + 4 * WIN_COL["mk"] + c
                step(ts(tiny_tmp[:, 28 + c:29 + c], colsA[:, k:k + 1], KSCALE, None, ALU.mult))

            mix_lo_to(4 * ADA[3] + 3)
            dve.wait_ge(S["z_taken"], Z_INDEX[("ada_col", 3)] + 1)
            step(tt(modc[:, 0:16, :], modc[:, 0:16, :], colsA[:, A_ADA:A_ADA + 16].unsqueeze(2).broadcast_to([P, 16, 2]), ALU.add))
            step(ts(sc1p, modc[:, 8:16, :], 1.0, None, ALU.add))
            for k in range(KD):
                for s, (t0, t1) in enumerate(SPANS):
                    ts(hT[:, k, t0:t1], hT[:, k, t0:t1], sc1p[:, k, s:s + 1], modc[:, k, s:s + 1], ALU.mult, ALU.add).then_inc(S["h_ready"], 1)
            dve.wait_ge(S["h_hi"], 1)
            step(tt(HL, hT, HH.bitcast(F32), ALU.subtract), "h_lo")

            dve.wait_ge(S["lam_exp"], 1)
            e = t[0]
            step(ts(t[1], nsp, 2.0, None, ALU.add))
            step(dve.reciprocal(t[1], t[1]))
            step(tt(e, nsp, t[1], ALU.mult))
            step(tt(t[1], e, e, ALU.mult))
            step(ts(t[2], t[1], 1.0 / 17, None, ALU.mult))
            for odd in (15, 13, 11, 9, 7, 5, 3):
                step(stt(t[2], t[2], 1.0 / odd, t[1], ALU.add, ALU.mult))
            step(stt(t[2], t[2], 1.0, e, ALU.add, ALU.mult))
            step(ts(t[1], lam, -1.0, 0.0, ALU.mult, ALU.max))
            step(stt(t[2], t[2], 2.0, t[1], ALU.mult, ALU.add))
            step(ts(nsp, t[2], -8.0, None, ALU.mult))
            step(ts(psp, t[2], 8.0, None, ALU.mult), "sp_ready")

            dve.wait_ge(S["z_taken"], Z_INDEX[("gates",)] + 1)
            dve.wait_ge(S["gate_w_in"], 32)
            step(tt(gz, gz, gbias.unsqueeze(1).broadcast_to([P, NT, 16]), ALU.add), "gz_ready")

            dve.wait_ge(S["z_taken"], Z_INDEX[("chan", "rx", C - 1)] + 1)
            for c in range(C):
                x, o = chunk(RX, c), chunk(XC, c)
                w = [colsA[:, A_CONVW + 4 * n + c:A_CONVW + 4 * n + c + 1] for n in range(4)]
                step(ts(o, x, w[2], colsA[:, A_CONVB + c:A_CONVB + c + 1], ALU.mult, ALU.add))
                for n, sh in ((0, -2), (1, -1), (3, 1)):
                    for s0, s1 in SPANS:
                        lo, hi = max(s0, s0 - sh), min(s1, s1 - sh)
                        step(stt(o[:, lo:hi], x[:, lo + sh:hi + sh], w[n], o[:, lo:hi], ALU.mult, ALU.add),
                             "rx_conv" if (c, n, s0) == (C - 1, 3, SEQ) else "dve")

            dve.wait_ge(S["z_taken"], Z_INDEX[("chan", "rg", C - 1)] + 1)
            for c in range(C):
                dve.wait_ge(S["lru_act"], 4 * c + 4)
                step(ts(LT, R_, 1.0, None, ALU.add))
                step(dve.reciprocal(LT, LT))
                step(stt(R_, R_, 0.0, LT, ALU.max, ALU.mult), "lru_den")
                for d in range(2):
                    step(tt(I_[:, d * T:(d + 1) * T], I_[:, d * T:(d + 1) * T], chunk(XC, c), ALU.mult))
                dve.wait_ge(S["lru_sqrt"], c + 1)
                step(tt(I_, I_, R_, ALU.mult))
                for d in range(2):
                    for s, (t0, t1) in enumerate(SPANS):
                        av, uv, hv = [z[:, d * T + t0:d * T + t1] for z in (A_, I_, HB)]
                        if d:
                            av, uv, hv = av[:, ::-1], uv[:, ::-1], hv[:, ::-1]
                        init = colsB[:, B_H0 + 4 * d + c:B_H0 + 4 * d + c + 1] if s else 0.0
                        step(dve.tensor_tensor_scan(hv, av, uv, init, ALU.mult, ALU.add))
                step(dve.tensor_copy(h_fin[:, 0, c:c + 1], HB[:, SEQ - 1:SEQ]))
                step(dve.tensor_copy(h_fin[:, 1, c:c + 1], HB[:, T:T + 1]))
                step(tt(LT[:, 0:T], HB[:, 0:T], HB[:, T:2 * T], ALU.add))
                step(tt(chunk(YR, c), chunk(YR, c), LT[:, 0:T], ALU.mult), "lru_done")

            dve.wait_ge(S["z_taken"], Z_INDEX[("chan", "gfb", C - 1)] + 1)
            for d, (f, kb) in enumerate(((FF, KBF), (FB, KBB))):
                for h in range(H):
                    k = 4 * d + h
                    step(ts(chunk(kb, h), chunk(f, h), neg_om_lb[:, k:k + 1], om_lb[:, k:k + 1], ALU.mult, ALU.add))
                    step(ts(chunk(f, h), chunk(f, h), om_lb[:, k:k + 1], lb[:, k:k + 1], ALU.mult, ALU.add))
                step(ts(f, f, TINY, None, ALU.max), "dve" if d == 0 else "hg_start")
            step(tt(QFB, QFF, FB, ALU.mult))
            dve.wait_ge(S["masks_cast"], 1)
            dve.wait_ge(S["consts_in"], 16)
            taken = [0]

            def scores_in():
                taken[0] += 1
                dve.wait_ge(S["hg_scores"], taken[0])
                return ps[:, 4 + (taken[0] - 1) % 4, :].rearrange("p (h t) -> p h t", h=H)

            for i in range(NT):
                step(tt(SCO[:, i], scores_in(), ident.unsqueeze(1).broadcast_to([P, H, P]), ALU.mult), "hg_taken")
            step(tt(QFF, QFF, FF, ALU.mult), "hg_level")

            for lv in range(LEVELS):
                h = 1 << lv
                units = 4 * ADA[max(LATE_ADA[lv + 1])] + 3 if LATE_ADA[lv + 1] else 0
                for i in range(NT):
                    for d in range(2):
                        m = hg_masks[:, d, lv, :].unsqueeze(1).broadcast_to([P, H, P])
                        step(dve.copy_predicated(SCO[:, i], m, scores_in()), "hg_taken")
                for q, kb, f, right_q in ((QFF, KBF, FF, 1), (QFB, KBB, FB, 0)):
                    qh, kh = halves(q, h), halves(kb, h)
                    fl = f[:, 0::2 * h].unsqueeze(2)
                    fr = f[:, h::2 * h].unsqueeze(2)
                    shape = [P, U // (2 * h), h]
                    first, last = (fl, fr) if right_q else (fr, fl)
                    step(tt(qh[right_q], qh[right_q], first.broadcast_to(shape), ALU.mult))
                    mix_lo_to(units, 1)
                    step(tt(kh[1 - right_q], kh[1 - right_q], last.broadcast_to(shape), ALU.mult))
                    mix_lo_to(units, 1)
                    step(tt(f[:, 0::2 * h], f[:, 0::2 * h], f[:, h::2 * h], ALU.mult), "dve" if right_q else "hg_level")
            assert not mix_todo
            for d in range(2):
                step(dve.tensor_copy(SCX[:, d], scores_in()), "hg_taken")
            for name, q, f, far, near in (("dve", QFF, FF, 2, 1), ("hg_final", QFB, FB, 1, 2)):
                qv = q.rearrange("p (h t) -> p h t", h=H)
                fv = f.rearrange("p (h t) -> p h t", h=H)
                step(tt(qv[:, :, far * P:(far + 1) * P], qv[:, :, far * P:(far + 1) * P],
                        fv[:, :, near * P:near * P + 1].broadcast_to([P, H, P]), ALU.mult), name)

            dve.wait_ge(S["z_taken"], Z_COUNT)
            step(tt(modc[:, 16:48, :], modc[:, 16:48, :], colsA[:, A_ADA + 16:A_ADA + 48].unsqueeze(2).broadcast_to([P, 32, 2]), ALU.add), "mod2_ready")
            dve.wait_ge(S["gz_rows"], 4)
            step(stt(FE, GF, -1.0, GF, ALU.mult, ALU.max), "f_abs")
            step(ts(GF, GF, 0.0, None, ALU.min))
            dve.wait_ge(S["f_ln"], 1)
            step(tt(GF, GF, FE, ALU.subtract))
            for d in range(2):
                for t0, t1 in SPANS:
                    src, dst = GF[:, d, t0:t1], BR[:, d, t0:t1]
                    if d:
                        src, dst = src[:, ::-1], dst[:, ::-1]
                    step(dve.tensor_tensor_scan(dst, src, zeros4[0:H, 0:t1 - t0], 0.0, ALU.add, ALU.add))
            step(tt(CR, GI, BR, ALU.subtract))
            dve.wait_ge(S["mini_in"], 48)
            for d in range(2):
                for s, (t0, t1) in enumerate(SPANS):
                    src, dst = CR[:, d, t0:t1], MR[:, d, t0:t1]
                    if d:
                        src, dst = src[:, ::-1], dst[:, ::-1]
                    step(dve.tensor_tensor_scan(dst, src, src, m0_rows[0:H, d:d + 1] if s else 0.0, ALU.max, ALU.max))
            step(stt(NBM, BR, -1.0, MR, ALU.mult, ALU.subtract))
            step(ts(m_fin[0:H, 0:1], NBM[:, 0, SEQ - 1:SEQ], -1.0, None, ALU.mult))
            step(ts(m_fin[0:H, 1:2], NBM[:, 1, 0:1], -1.0, None, ALU.mult), "m_rows")

            for h in range(H):
                dve.wait_ge(S["o_std"], h + 1)
                b = h % 2
                step(dve.reciprocal(O_STD[:, b, :], O_STD[:, b, :]))
                step(tt(O_STD[:, b, :], ps[:, 4 + h, 0:T], O_STD[:, b, :], ALU.mult))
                step(stt(chunk(YH, h), O_STD[:, b, :], colsA[:, A_HGG + h:A_HGG + h + 1], chunk(YH, h), ALU.mult, ALU.mult), "o_norm")

            def weights_of(n):
                h, d, b = n // 2, n % 2, n % 2
                dve.wait_ge(S["bc_ready"], n + 1)
                dve.wait_ge(S["si_ready"], n + 1)
                m = ps[:, 0, :]
                pw_ = PW_[:, b, :]
                parts = [(0, 0, P, 0)] + ([(P, P, T, 1), (3 * P, 2 * P, T, 2)] if d == 0 else [(P, P, 2 * P, 1), (2 * P, P, T, 2)])
                for k, (o, t0, t1, i) in enumerate(parts):
                    step(ts(pw_[:, o:o + t1 - t0], m[:, t0:t1], c_cols[:, d, i, h:h + 1], 0.0, ALU.subtract, ALU.max),
                         "p_arg" if k == 2 else "dve")
                step(tt(QS[:, b, :], chunk(MQ, h)[:, SEQ:T], SI[:, b, :], ALU.mult), "qs_ready")
                dve.wait_ge(S["p_exp"], n + 1)
                last = 0 if d else P - 1
                step(ts(KE[:, b, :], KTOK[:, h * P:(h + 1) * P], pw_[:, last:last + 1], None, ALU.mult), "ke_ready")
                dve.wait_ge(S["p_mask"], 2 * n + 2)
                dve.wait_ge(S["ml_scores"], n + 1)
                step(tt(WW[:, b, :], pw_, ps[:, 2, :], ALU.mult), "w_ready")

            dve.wait_ge(S["c_cols"], 1)
            dve.wait_ge(S["kT_sb"], 1)
            weights_of(0)
            for n in range(10):
                h, d = n // 2, n % 2
                b = n % 2
                if n < 7:
                    weights_of(n + 1)
                if d == 0 and n:
                    dve.wait_ge(S["hm_ready"], h)
                    step(tt(HT2[:, 0, :], HS[:, 1, :], ps[:, 6, 0:T], ALU.subtract), "hc_ready")
                if d == 1 and n > 1:
                    dve.wait_ge(S["hstd_ready"], h)
                    step(dve.reciprocal(HT2[:, 1, :], HT2[:, 1, :]))
                    step(tt(HT2[:, 1, :], HT2[:, 1, :], HT2[:, 0, :], ALU.mult))
                    step(stt(chunk(YM, h - 1), HT2[:, 1, :], colsA[:, A_MLG + h - 1:A_MLG + h], chunk(YM, h - 1), ALU.mult, ALU.mult),
                         "ml_done" if h == H else "dve")
                if n < 8:
                    dve.wait_ge(S["num_ready"], n + 1)
                    dve.wait_ge(S["den_abs"], n + 1)
                    step(tt(DEN[:, b, :], DEN[:, b, :], FLOOR[:, b, :], ALU.max))
                    step(dve.reciprocal(DEN[:, b, :], DEN[:, b, :]))
                    if d == 0:
                        step(tt(HS[:, 0, :], ps[:, 4, 0:T], DEN[:, b, :], ALU.mult), "h_done")
                    else:
                        step(tt(DEN[:, b, :], ps[:, 4, 0:T], DEN[:, b, :], ALU.mult))
                        step(tt(HS[:, 1, :], HS[:, 0, :], DEN[:, b, :], ALU.add), "h_done")

            def norm(i, v, name, last="dve"):
                x = X1[:, i, :]
                for half in range(2):
                    step(dve.bn_stats(mv_stats[:, 6 * half:6 * half + 6], x[:, half * 512:(half + 1) * 512]))
                step(dve.bn_aggr(mv_stats[:, 12:14], mv_stats[:, 0:12]), name + "_var")
                dve.wait_ge(S[name + "_std"], i + 1)
                step(dve.reciprocal(rstd, rstd))
                step(stt(x, x, mv_stats[:, 12:13], ln_b[:, v, :], ALU.subtract, ALU.mult))
                step(stt(x, x, rstd, ln_b[:, v + 1, :], ALU.mult, ALU.add), last)

            dve.wait_ge(S["x2_in"], 32)
            dve.wait_ge(S["pos2_in"], 16)
            step(tt(X1[:, 1:3, :], X1[:, 1:3, :], pos2, ALU.add))
            dve.wait_ge(S["ln_in"], 16 * 8)
            dve.wait_ge(S["bcast_taken"], 16)
            for i in range(NT):
                s = min(i, 1)
                dve.wait_ge(S["y_ready"], 2 * i + 2)
                for half in range(2):
                    cols = slice(half * 512, (half + 1) * 512)
                    step(tt(H2[:, i, cols], ps[:, 2 * i + half, :], g1_b[:, s, cols], ALU.mult))
                step(stt(X1[:, i, :], X1[:, i, :], ALPHA, H2[:, i, :], ALU.mult, ALU.add))
                norm(i, 0, "ln")
                step(tt(H2[:, i, :], X1[:, i, :], sc2_b[:, s, :], ALU.mult))
                step(tt(H2[:, i, :], H2[:, i, :], sh2_b[:, s, :], ALU.add), "h2_ready")
                dve.wait_ge(S["h2_hi"], i + 1)
                step(tt(H2L[:, i, :], H2[:, i, :], H2H[:, i, :].bitcast(F32), ALU.subtract), "h2_lo")

            def over3(x, n=NE):
                return x.unsqueeze(2).broadcast_to([P, NT, n])

            step(dve.memset(YACC, 0.0))
            dve.wait_ge(S["logits_ready"], 1)
            logits = ps[:, 0, 0:48].rearrange("p (i e) -> p i e", i=NT)
            step(dve.tensor_reduce(r3[0], logits, AX.X, ALU.max))
            step(tt(scores, logits, over3(r3[0]), ALU.subtract), "smax_ready")
            dve.wait_ge(S["sexp_ready"], 1)
            step(dve.tensor_reduce(r3[1], scores, AX.X, ALU.add))
            step(dve.reciprocal(r3[2], r3[1]))
            step(tt(scores, scores, over3(r3[2]), ALU.mult))
            step(tt(sel, scores, b_router.unsqueeze(1).broadcast_to([P, NT, NE]), ALU.add))
            sv = sel.rearrange("p i (g e) -> p i g e", g=NG)
            e0, e1, e2, e3 = [sv[:, :, :, n] for n in range(4)]
            step(tt(g12[0], e0, e1, ALU.max))
            step(tt(g12[1], e0, e1, ALU.min))
            step(tt(g12[2], e2, e3, ALU.max))
            step(tt(g12[3], e2, e3, ALU.min))
            step(tt(g12[4], g12[0], g12[2], ALU.max))
            step(tt(g12[5], g12[0], g12[2], ALU.min))
            step(tt(g12[6], g12[1], g12[3], ALU.max))
            step(tt(g12[5], g12[5], g12[6], ALU.max))
            step(tt(g12[4], g12[4], g12[5], ALU.add))

            def first_max(out, x, tmp, n):
                step(dve.tensor_reduce(r3[3], x, AX.X, ALU.max))
                step(tt(tmp, x, over3(r3[3], n), ALU.is_equal))
                step(tt(tmp, tmp, desc16[:, 0:n].unsqueeze(1).broadcast_to([P, NT, n]), ALU.mult))
                step(dve.tensor_reduce(r3[4], tmp, AX.X, ALU.max))
                step(tt(out, tmp, over3(r3[4], n), ALU.is_equal))

            first_max(g12[0], g12[4], g12[1], NG)
            step(ts(g12[1], g12[0], BIG, -BIG, ALU.mult, ALU.add))

            def per_expert(x):
                return x.unsqueeze(3).broadcast_to([P, NT, NG, NG])

            def grouped(x):
                return x.rearrange("p i (g e) -> p i g e", g=NG)

            step(tt(grouped(masked), sv, per_expert(g12[0]), ALU.mult))
            step(tt(grouped(masked), grouped(masked), per_expert(g12[1]), ALU.add))
            first_max(oh1, masked, t16a, NE)
            step(stt(masked, oh1, -3e38, masked, ALU.mult, ALU.add))
            first_max(oh2, masked, t16a, NE)
            step(tt(mask, oh1, oh2, ALU.add), "mask_ready")
            step(tt(comb, scores, mask, ALU.mult))
            step(dve.tensor_reduce(r3[1], comb, AX.X, ALU.add))
            step(dve.reciprocal(r3[2], r3[1]))
            step(tt(PW[:, :, :, 1].rearrange("p e i -> p i e"), comb, over3(r3[2]), ALU.mult))
            dve.wait_ge(S["ranks_ready"], 1)
            step(tt(ranks, ps[:, 1, 0:48].rearrange("p (i e) -> p i e", i=NT), mask, ALU.mult))
            step(ts(t16a, mask, 4096.0, -4096.0, ALU.mult, ALU.add))
            step(tt(PW[:, :, :, 0].rearrange("p e i -> p i e"), ranks, t16a, ALU.add))
            step(dve.tensor_reduce(over_f[:, 0:1], ps[:, 1, 48:64], AX.X, ALU.max))
            step(dve.tensor_copy(over_i[:, 0:1], over_f[:, 0:1]), "route_ready")

            def select(n, e):
                dve.tensor_copy(pw, PW[:, bass.ds(e, 1)].rearrange("p a i w -> p (a i) w")).then_inc(S["sel_cols"], 1)
                dve.wait_ge(S["sel_cols"], n + 1)
                for i in range(NT):
                    ins = ts(Sel[:, i, :], iota, pw[:, i, 0:1], None, ALU.is_equal)
                ins.then_inc(S["sel_ready"], 1)

            def gated(n):
                dve.wait_ge(S["sg_ready"], n + 1)
                dve.wait_ge(S["unit_used"], 12 * n + (MIX_USED + 8))
                stt(AC, SG, slot_w, ps[:, 4, :], ALU.mult, ALU.mult).then_inc(S["act_ready"], 1)

            def gather_lo(n):
                for half in range(2):
                    dve.wait_ge(S["gather_taken"], 3 * n + (half + 2))
                    sl = slice(4 * half, 4 * half + 4)
                    tt(HGL[:, sl, :], ps[:, half, :].rearrange("p (k j) -> p k j", k=4), HGH[:, sl, :].bitcast(F32),
                       ALU.subtract).then_inc(S["hg_lo"], 1)

            def act_lo(n):
                dve.wait_ge(S["act_T_sb"], n + 1)
                tt(ACL, ps[:, 3, :].rearrange("p (k j) -> p k j", k=C), ACH.bitcast(F32), ALU.subtract).then_inc(S["act_lo"], 1)

            def down_lo(n):
                for half in range(2):
                    dve.wait_ge(S["down_sb"], 2 * n + (half + 1))
                    tt(DNL[:, half, :], ps[:, 5 + half, :], DNH[:, half, :].bitcast(F32), ALU.subtract).then_inc(S["down_lo"], 1)

            def expert_lo(n, j, quarters=range(4)):
                for q in quarters:
                    if q not in POOL_Q[j]:
                        dve.wait_ge(S["hi_ready"], 12 * n + (MIX_UNITS + 4 * j + q + 1))
                        tt(w_lo[:, q, :], raw_unit((FIRST_EXPERT + j) % NSLOT, q, False), w_hi[:, q, :].bitcast(F32),
                           ALU.subtract).then_inc(S["lo_dve"], 1)

            def add_back(n, parts=range(6)):
                for r in parts:
                    i, half = r // 2, r % 2
                    dve.wait_ge(S["scattered"], 6 * n + (r + 1))
                    yv = YACC[:, i, half * 512:(half + 1) * 512]
                    tt(yv, yv, ps[:, (7, 2)[r % 2], :], ALU.add).then_inc(S["y_added"], 1)

            def expert(n, next_e, before):
                if next_e is not None:
                    dve.wait_ge(S["gathered"], n + 1)
                    select(n + 1, next_e)
                expert_lo(n, 1)
                if before:
                    add_back(n - 1)
                expert_lo(n, 2, (0, 1))
                gated(n)
                expert_lo(n, 2, (2, 3))
                act_lo(n)
                if next_e is not None:
                    expert_lo(n + 1, 0, (0,))
                    gather_lo(n + 1)
                    expert_lo(n + 1, 0, (1, 2, 3))
                down_lo(n)

            def expert_pass(base):
                select(base, 0)
                expert_lo(base, 0)
                gather_lo(base)
                expert(base, 1, False)
                with dve.Fori(0, NPAIR - 1) as i:
                    for m in (1, 2):
                        expert(2 * i + (base + m), 2 * i + (m + 1), True)
                expert(base + NE - 1, None, True)
                add_back(base + NE - 1)

            expert_pass(0)
            over = dve.value_load(over_i[0:1, 0:1], min_val=0, max_val=T)
            with dve.If(over > P):
                for base in (NE, 2 * NE):
                    dve.wait_ge(S["gathered"], base)
                    ts(PW[:, :, :, 0], PW[:, :, :, 0], -float(P), None, ALU.add).then_inc(S["over_shift"], 1)
                    dve.wait_ge(S["over_shift"], base // NE)
                    expert_pass(base)

            dve.wait_ge(S["g2_moved"], 1)
            for i in range(NT):
                s = min(i, 1)
                step(tt(YACC[:, i, :], YACC[:, i, :], g2_b[:, s, :], ALU.mult))
                step(stt(X1[:, i, :], X1[:, i, :], ALPHA, YACC[:, i, :], ALU.mult, ALU.add))
                norm(i, 2, "ln2", "out_tile")


_INS = ["x_prompt", "x_sample", "state_lru_h", "state_hgrn_S", "state_mlstm_C", "state_mlstm_n", "state_mlstm_m", "c", "c_ctx",
        "w_ada", "b_ada", "w_in", "b_in", "conv_w", "conv_b", "lru_wa", "lru_ba", "lru_wx", "lru_bx", "lru_lam", "hg_lb",
        "hg_norm_g", "ml_norm_g", "w_out", "ln1_g", "ln1_b", "ln2_g", "ln2_b", "w_router", "b_router", "w_gate", "w_up", "w_down"]
_OUTS = [(1, SEQ, D), (1, LAT, D), (1, 1, 2, G), (1, 1, 2, H, P, P), (1, 1, 2, H, P, P), (1, 1, 2, H, P), (1, 1, 2, H)]


def _constants():
    import numpy as np

    r = np.arange(P)
    consts = np.zeros((P, 400), np.float32)
    consts[:, 0:128] = r[:, None] == r[None, :]
    consts[:, 128:256] = r[:, None] < r[None, :]
    consts[:, 256:384] = r[None, :]
    consts[:, 384:400] = 16 - np.arange(16)[None, :]
    masks = np.zeros((P, 2, LEVELS, P), np.float32)
    for lv in range(LEVELS):
        same = (r[:, None] >> (lv + 1)) == (r[None, :] >> (lv + 1))
        left = ((r >> lv) & 1) == 0
        masks[:, 0, lv] = same & left[:, None] & ~left[None, :]
        masks[:, 1, lv] = same & ~left[:, None] & left[None, :]
    q = D // 4
    freq = np.exp(np.float32(-np.log(10000.0)) * np.arange(q, dtype=np.float32) / np.float32(q)).astype(np.float32)
    tok = np.arange(LAT)
    ar = (tok // 64).astype(np.float32)[:, None] * freq
    ac = (tok % 64).astype(np.float32)[:, None] * freq
    pos = np.concatenate([np.sin(ar), np.cos(ar), np.sin(ac), np.cos(ac)], axis=-1).astype(np.float32)
    return {"consts": consts, "hg_masks": masks.reshape(P, -1), "pos": pos}


def kernel(**inputs):
    import numpy as _np
    import concourse.bacc as _bacc
    from concourse import mybir as _mybir
    from concourse.bass_utils import run_bass_kernel_spmd as _run

    nc = _bacc.Bacc("TRN2", target_bir_lowering=False, num_devices=1)
    arrays, args = {}, {}
    named = {name: _np.ascontiguousarray(inputs[name]) for name in _INS}
    named.update(_constants())
    for name, value in named.items():
        arrays[f"in_{name}"] = value
        args[name] = nc.dram_tensor(f"in_{name}", value.shape, _mybir.dt.from_np(value.dtype), kind="ExternalInput").ap()
    outs = [nc.dram_tensor(f"out_{i}", shape, _mybir.dt.float32, kind="ExternalOutput").ap() for i, shape in enumerate(_OUTS)]
    build(nc, args, outs)
    r = _run(nc, [arrays], core_ids=[0])
    return tuple(r.results[0][f"out_{i}"] for i in range(len(_OUTS)))
```
